# Optimizing a Trainium2 kernel written in Bass

```python
import jax, jax.numpy as jnp
from jax import lax
import numpy as np

D_MODEL = 1024
BATCH = 1
SEQ = 1024
DEPTH = 1
DEC_BATCH = 8
DEC_SEQ = 4
PAST_LEN = 2048
PAGE_SIZE = 128

HEAD_DIM = 64
A_HEADS = 8
A_WIDTH = A_HEADS * HEAD_DIM
B_HEADS = 8
B_KV_HEADS = 2
B_GROUP = B_HEADS // B_KV_HEADS
B_WIDTH = B_HEADS * HEAD_DIM
B_KV_WIDTH = B_KV_HEADS * HEAD_DIM
MIX_WIDTH = A_WIDTH + B_WIDTH
DECAY_LORA = 64
ICLR_LORA = 64
GATE_LORA = 128
SHIFT_W = 3 * A_WIDTH + DECAY_LORA + ICLR_LORA + GATE_LORA
IN_W = SHIFT_W + B_WIDTH + 2 * B_KV_WIDTH
WINDOW = 128
ATTN_BLOCK = 128
N_GROUPS = 4
EXPERTS_PER_GROUP = 4
N_EXPERTS = N_GROUPS * EXPERTS_PER_GROUP
TOP_K_INNER = 2
EXPERT_FF = 512
MOE_BLOCK = 128
RMS_EPS = 1e-6
LNX_EPS = 64e-5
DECAY_OFFSET = 0.5

kernel_name = "hymba_rwkv7_swa_sink_hiermoe_step"

def rmsnorm(x, g):
    x32 = x.astype(jnp.float32)
    y = x32 * lax.rsqrt(jnp.mean(x32 * x32, axis=-1, keepdims=True) + RMS_EPS)
    return (y * g.astype(jnp.float32)).astype(x.dtype)

def alibi_slopes():
    h = jnp.arange(1, B_HEADS + 1, dtype=jnp.float32)
    return jnp.exp2(-8.0 * h / B_HEADS).reshape(B_KV_HEADS, B_GROUP)

def sink_probs(scores, mask, sink):
    scores = jnp.where(mask, scores, -jnp.inf)
    sk = sink.astype(jnp.float32).reshape(B_KV_HEADS, B_GROUP, 1, 1)
    m = jnp.maximum(jnp.max(scores, axis=-1, keepdims=True), sk)
    p = jnp.exp(scores - m)
    denom = jnp.sum(p, axis=-1, keepdims=True) + jnp.exp(sk - m)
    return p / denom

def swa_prompt(q, k, v, sink):
    Bn, T = q.shape[0], q.shape[1]
    nb = T // ATTN_BLOCK
    scale = HEAD_DIM ** -0.5
    qb = q.reshape(Bn, nb, ATTN_BLOCK, B_KV_HEADS, B_GROUP, HEAD_DIM)
    pad = jnp.zeros((Bn, ATTN_BLOCK, B_KV_HEADS, HEAD_DIM), k.dtype)
    kb = jnp.concatenate([pad, k], axis=1).reshape(Bn, nb + 1, ATTN_BLOCK, B_KV_HEADS, HEAD_DIM)
    vb = jnp.concatenate([pad.astype(v.dtype), v], axis=1).reshape(Bn, nb + 1, ATTN_BLOCK, B_KV_HEADS, HEAD_DIM)
    keys = jnp.concatenate([kb[:, :-1], kb[:, 1:]], axis=2)
    vals = jnp.concatenate([vb[:, :-1], vb[:, 1:]], axis=2)
    s = jnp.einsum('bnqkgd,bnskd->bnkgqs', qb, keys, preferred_element_type=jnp.float32) * scale
    dist = jnp.arange(ATTN_BLOCK)[:, None] + ATTN_BLOCK - jnp.arange(2 * ATTN_BLOCK)[None, :]
    kpos = jnp.arange(nb)[:, None] * ATTN_BLOCK - ATTN_BLOCK + jnp.arange(2 * ATTN_BLOCK)[None, :]
    mask = ((dist >= 0) & (dist < WINDOW))[None, None, None, None] & (kpos >= 0)[None, :, None, None, None, :]
    s = s - alibi_slopes()[:, :, None, None] * dist.astype(jnp.float32)
    p = sink_probs(s, mask, sink)
    o = jnp.einsum('bnkgqs,bnskd->bnqkgd', p.astype(vals.dtype), vals).reshape(Bn, T, B_WIDTH)
    return o, k[:, -WINDOW:], v[:, -WINDOW:]

def swa_sample(q, k, v, sink, win_k, win_v):
    Bn, T = q.shape[0], q.shape[1]
    Wb = win_k.shape[1]
    scale = HEAD_DIM ** -0.5
    keys = jnp.concatenate([win_k.astype(k.dtype), k], axis=1)
    vals = jnp.concatenate([win_v.astype(v.dtype), v], axis=1)
    qg = q.reshape(Bn, T, B_KV_HEADS, B_GROUP, HEAD_DIM)
    s = jnp.einsum('btkgd,bskd->bkgts', qg, keys, preferred_element_type=jnp.float32) * scale
    dist = jnp.arange(T)[:, None] + Wb - jnp.arange(Wb + T)[None, :]
    mask = (dist >= 0) & (dist < WINDOW)
    s = s - alibi_slopes()[:, :, None, None] * dist.astype(jnp.float32)
    p = sink_probs(s, mask, sink)
    o = jnp.einsum('bkgts,bskd->btkgd', p.astype(vals.dtype), vals).reshape(Bn, T, B_WIDTH)
    return o, keys[:, -Wb:], vals[:, -Wb:]

def rwkv_scan(S0, r, w, k, v, kk, a):
    def step(S, inp):
        r_t, w_t, k_t, v_t, kk_t, a_t = inp
        sa = jnp.einsum('bhvk,bhk->bhv', S, kk_t)
        S = S * w_t[:, :, None, :] - sa[..., None] * (kk_t * a_t)[:, :, None, :] + v_t[..., None] * k_t[:, :, None, :]
        y = jnp.einsum('bhvk,bhk->bhv', S, r_t)
        return S, y
    xs = (jnp.swapaxes(r, 0, 1), jnp.swapaxes(w, 0, 1), jnp.swapaxes(k, 0, 1),
          jnp.swapaxes(v, 0, 1), jnp.swapaxes(kk, 0, 1), jnp.swapaxes(a, 0, 1))
    S, ys = lax.scan(step, S0, xs)
    return S, jnp.swapaxes(ys, 0, 1)

def rwkv_mixer(pa, shift_prev, S0, prm):
    Bn, T = pa.shape[0], pa.shape[1]
    f32 = jnp.float32
    pa_prev = jnp.concatenate([shift_prev[:, None, :].astype(pa.dtype), pa[:, :-1]], axis=1)
    xm = (pa + prm['mu_shift'] * (pa_prev - pa)).astype(f32)
    c = np.cumsum([A_WIDTH, A_WIDTH, A_WIDTH, DECAY_LORA, ICLR_LORA])
    r, k, v, wd, ad, gd = jnp.split(xm, [int(i) for i in c], axis=-1)
    w_log = -jax.nn.softplus(-(prm['w_decay0'] + jnp.tanh(wd) @ prm['w_decay_up'])) - DECAY_OFFSET
    decay = jnp.exp(-jnp.exp(w_log))
    a = jax.nn.sigmoid(prm['w_iclr0'] + ad @ prm['w_iclr_up'])
    g = jax.nn.sigmoid(gd) @ prm['w_gate_up']
    kk = (k * prm['k_k']).reshape(Bn, T, A_HEADS, HEAD_DIM)
    kk = kk * lax.rsqrt(jnp.maximum(jnp.sum(kk * kk, axis=-1, keepdims=True), 1e-24))
    k = k * (1.0 + (a - 1.0) * prm['k_a'])
    hs = (Bn, T, A_HEADS, HEAD_DIM)
    rh, kh, vh = r.reshape(hs), k.reshape(hs), v.reshape(hs)
    S, y = rwkv_scan(S0.astype(f32), rh, decay.reshape(hs), kh, vh, kk, a.reshape(hs))
    mu = jnp.mean(y, axis=-1, keepdims=True)
    var = jnp.mean(jnp.square(y - mu), axis=-1, keepdims=True)
    yn = ((y - mu) * lax.rsqrt(var + LNX_EPS)).reshape(Bn, T, A_WIDTH) * prm['lnx_g'] + prm['lnx_b']
    bonus = (jnp.sum(rh * kh * prm['r_k'], axis=-1, keepdims=True) * vh).reshape(Bn, T, A_WIDTH)
    out = (yn + bonus) * g
    return out, S, pa[:, -1]

def hier_moe(h, prm):
    T = h.shape[0]
    h32 = h.astype(jnp.float32)
    pg = jax.nn.softmax(h32 @ prm['w_route_group'] + prm['b_route_group'], axis=-1)
    g_idx = jnp.argmax(pg, axis=-1)
    g_w = jnp.take_along_axis(pg, g_idx[:, None], axis=-1)
    le = (h32 @ prm['w_route_expert'] + prm['b_route_expert']).reshape(T, N_GROUPS, EXPERTS_PER_GROUP)
    le_g = jnp.take_along_axis(le, g_idx[:, None, None], axis=1)[:, 0]
    top_p, top_i = lax.top_k(jax.nn.softmax(le_g, axis=-1), TOP_K_INNER)
    wts = g_w * top_p / jnp.sum(top_p, axis=-1, keepdims=True)
    e_idx = g_idx[:, None] * EXPERTS_PER_GROUP + top_i
    A = T * TOP_K_INNER
    flat_e = e_idx.reshape(A).astype(jnp.int32)
    flat_w = wts.reshape(A)
    flat_tok = jnp.repeat(jnp.arange(T, dtype=jnp.int32), TOP_K_INNER)
    order = jnp.argsort(flat_e)
    se, stok, sw = flat_e[order], flat_tok[order], flat_w[order]
    counts = jnp.bincount(flat_e, length=N_EXPERTS)
    starts = jnp.cumsum(counts) - counts
    padded = (counts + MOE_BLOCK - 1) // MOE_BLOCK * MOE_BLOCK
    pend = jnp.cumsum(padded)
    pstarts = pend - padded
    dest = pstarts[se] + (jnp.arange(A, dtype=jnp.int32) - starts[se])
    n_blocks = -(-A // MOE_BLOCK) + N_EXPERTS
    P = n_blocks * MOE_BLOCK
    xbuf = jnp.zeros((P, h.shape[1]), h.dtype).at[dest].set(h[stok])
    block_e = jnp.clip(jnp.searchsorted(pend, jnp.arange(n_blocks) * MOE_BLOCK, side='right'), 0, N_EXPERTS - 1)
    w_gate, w_up, w_down = prm['w_exp_gate'], prm['w_exp_up'], prm['w_exp_down']

    def expert_block(args):
        xb, e = args
        return (jax.nn.silu(xb @ w_gate[e]) * (xb @ w_up[e])) @ w_down[e]

    ybuf = lax.map(expert_block, (xbuf.reshape(n_blocks, MOE_BLOCK, h.shape[1]), block_e)).reshape(P, -1)
    y = jnp.zeros((T, ybuf.shape[1]), ybuf.dtype).at[stok].add(ybuf[dest] * sw[:, None].astype(ybuf.dtype))
    return y

def trunk_layer(x, shift_prev, S0, win_k, win_v, prm):
    Bn, T, D = x.shape
    h = rmsnorm(x, prm['norm_mix_g'])
    p = h @ prm['w_in']
    pa = p[..., :SHIFT_W]
    pb = p[..., SHIFT_W:]
    o_a, S_new, shift_new = rwkv_mixer(pa, shift_prev, S0, prm)
    q = pb[..., :B_WIDTH].reshape(Bn, T, B_HEADS, HEAD_DIM)
    k = pb[..., B_WIDTH:B_WIDTH + B_KV_WIDTH].reshape(Bn, T, B_KV_HEADS, HEAD_DIM)
    v = pb[..., B_WIDTH + B_KV_WIDTH:].reshape(Bn, T, B_KV_HEADS, HEAD_DIM)
    if win_k is None:
        o_b, kbuf, vbuf = swa_prompt(q, k, v, prm['attn_sink'])
    else:
        o_b, kbuf, vbuf = swa_sample(q, k, v, prm['attn_sink'], win_k, win_v)
    o_b = rmsnorm(o_b, prm['attn_norm_g'])
    mixed = jnp.concatenate([o_a.astype(x.dtype), o_b.astype(x.dtype)], axis=-1)
    x = x + (mixed @ prm['w_out']).astype(x.dtype)
    h2 = rmsnorm(x, prm['norm_ffn_g'])
    x = x + hier_moe(h2.reshape(Bn * T, D), prm).reshape(Bn, T, D).astype(x.dtype)
    return x, S_new, shift_new, kbuf, vbuf

def setup_inputs(seed: int = 0) -> dict:
    key = jax.random.key(seed)
    ks = jax.random.split(key, 32)
    f32 = jnp.float32
    L = DEPTH
    win_buf = min(WINDOW, PAST_LEN)

    def nrm(k, shape, scale):
        return jax.random.normal(k, shape, f32) * scale

    return {
        "x_prompt": nrm(ks[0], (BATCH, SEQ, D_MODEL), 1.0),
        "x_sample": nrm(ks[1], (DEC_BATCH, DEC_SEQ, D_MODEL), 1.0),
        "state_rwkv": nrm(ks[2], (L, DEC_BATCH, A_HEADS, HEAD_DIM, HEAD_DIM), 0.5),
        "state_shift": nrm(ks[3], (L, DEC_BATCH, SHIFT_W), 1.0),
        "cache_win_k": nrm(ks[4], (L, DEC_BATCH, win_buf, B_KV_HEADS, HEAD_DIM), 1.0),
        "cache_win_v": nrm(ks[5], (L, DEC_BATCH, win_buf, B_KV_HEADS, HEAD_DIM), 1.0),
        "norm_mix_g": 1.0 + nrm(ks[6], (L, D_MODEL), 0.02),
        "w_in": nrm(ks[7], (L, D_MODEL, IN_W), D_MODEL ** -0.5),
        "mu_shift": jax.random.uniform(ks[8], (L, SHIFT_W), f32),
        "w_decay0": jax.random.uniform(ks[9], (L, A_WIDTH), f32, -6.0, -1.0),
        "w_decay_up": nrm(ks[10], (L, DECAY_LORA, A_WIDTH), DECAY_LORA ** -0.5),
        "w_iclr0": nrm(ks[11], (L, A_WIDTH), 0.1),
        "w_iclr_up": nrm(ks[12], (L, ICLR_LORA, A_WIDTH), ICLR_LORA ** -0.5),
        "w_gate_up": nrm(ks[13], (L, GATE_LORA, A_WIDTH), GATE_LORA ** -0.5),
        "k_k": 0.85 + nrm(ks[14], (L, A_WIDTH), 0.02),
        "k_a": 1.0 + nrm(ks[15], (L, A_WIDTH), 0.02),
        "r_k": nrm(ks[16], (L, A_HEADS, HEAD_DIM), 0.1),
        "lnx_g": 1.0 + nrm(ks[17], (L, A_WIDTH), 0.02),
        "lnx_b": nrm(ks[18], (L, A_WIDTH), 0.02),
        "attn_sink": nrm(ks[19], (L, B_HEADS), 0.5),
        "attn_norm_g": 1.0 + nrm(ks[20], (L, B_WIDTH), 0.02),
        "w_out": nrm(ks[21], (L, MIX_WIDTH, D_MODEL), MIX_WIDTH ** -0.5),
        "norm_ffn_g": 1.0 + nrm(ks[22], (L, D_MODEL), 0.02),
        "w_route_group": nrm(ks[23], (L, D_MODEL, N_GROUPS), D_MODEL ** -0.5),
        "b_route_group": nrm(ks[24], (L, N_GROUPS), 0.01),
        "w_route_expert": nrm(ks[25], (L, D_MODEL, N_EXPERTS), D_MODEL ** -0.5),
        "b_route_expert": nrm(ks[26], (L, N_EXPERTS), 0.01),
        "w_exp_gate": nrm(ks[27], (L, N_EXPERTS, D_MODEL, EXPERT_FF), D_MODEL ** -0.5),
        "w_exp_up": nrm(ks[28], (L, N_EXPERTS, D_MODEL, EXPERT_FF), D_MODEL ** -0.5),
        "w_exp_down": nrm(ks[29], (L, N_EXPERTS, EXPERT_FF, D_MODEL), EXPERT_FF ** -0.5),
        "norm_final_g": 1.0 + nrm(ks[30], (D_MODEL,), 0.02),
    }

def reference(x_prompt, x_sample, state_rwkv, state_shift, cache_win_k, cache_win_v,
              norm_mix_g, w_in, mu_shift, w_decay0, w_decay_up, w_iclr0, w_iclr_up, w_gate_up,
              k_k, k_a, r_k, lnx_g, lnx_b, attn_sink, attn_norm_g, w_out, norm_ffn_g,
              w_route_group, b_route_group, w_route_expert, b_route_expert,
              w_exp_gate, w_exp_up, w_exp_down, norm_final_g):
    xp, xs = x_prompt, x_sample
    Bp = xp.shape[0]
    rwkv_p, shift_p, kp_list, vp_list = [], [], [], []
    rwkv_s, shift_s, ks_list, vs_list = [], [], [], []
    for l in range(DEPTH):
        prm = dict(norm_mix_g=norm_mix_g[l], w_in=w_in[l], mu_shift=mu_shift[l], w_decay0=w_decay0[l],
                   w_decay_up=w_decay_up[l], w_iclr0=w_iclr0[l], w_iclr_up=w_iclr_up[l], w_gate_up=w_gate_up[l],
                   k_k=k_k[l], k_a=k_a[l], r_k=r_k[l], lnx_g=lnx_g[l], lnx_b=lnx_b[l], attn_sink=attn_sink[l],
                   attn_norm_g=attn_norm_g[l], w_out=w_out[l], norm_ffn_g=norm_ffn_g[l],
                   w_route_group=w_route_group[l], b_route_group=b_route_group[l],
                   w_route_expert=w_route_expert[l], b_route_expert=b_route_expert[l],
                   w_exp_gate=w_exp_gate[l], w_exp_up=w_exp_up[l], w_exp_down=w_exp_down[l])
        shift0 = jnp.zeros((Bp, SHIFT_W), xp.dtype)
        S0 = jnp.zeros((Bp, A_HEADS, HEAD_DIM, HEAD_DIM), jnp.float32)
        xp, S_p, sh_p, k_p, v_p = trunk_layer(xp, shift0, S0, None, None, prm)
        xs, S_s, sh_s, k_s, v_s = trunk_layer(xs, state_shift[l], state_rwkv[l], cache_win_k[l], cache_win_v[l], prm)
        rwkv_p.append(S_p); shift_p.append(sh_p); kp_list.append(k_p); vp_list.append(v_p)
        rwkv_s.append(S_s); shift_s.append(sh_s); ks_list.append(k_s); vs_list.append(v_s)
    y_prompt = rmsnorm(xp, norm_final_g)
    y_sample = rmsnorm(xs, norm_final_g)
    state_rwkv_prompt = jnp.stack(rwkv_p, axis=0)
    state_shift_prompt = jnp.stack(shift_p, axis=0)
    cache_win_k_prompt = jnp.stack(kp_list, axis=0)
    cache_win_v_prompt = jnp.stack(vp_list, axis=0)
    state_rwkv_sample = jnp.stack(rwkv_s, axis=0)
    state_shift_sample = jnp.stack(shift_s, axis=0)
    cache_win_k_sample = jnp.stack(ks_list, axis=0)
    cache_win_v_sample = jnp.stack(vs_list, axis=0)
    return (y_prompt, y_sample, state_rwkv_prompt, state_shift_prompt, cache_win_k_prompt, cache_win_v_prompt,
            state_rwkv_sample, state_shift_sample, cache_win_k_sample, cache_win_v_sample)


_drawn_inputs = setup_inputs


def setup_inputs(seed=0):
    import zlib

    import numpy as np

    out = dict(_drawn_inputs(seed))
    spreads = {}
    factors = {'k_k': 2.988,
     'k_a': 2.674,
     'lnx_g': 5.388,
     'lnx_b': 6.209,
     'attn_norm_g': 3.136,
     'norm_ffn_g': 2.907,
     'b_route_group': 5.874,
     'b_route_expert': 8.0,
     'norm_final_g': 2.746}
    for name, (base, spread) in spreads.items():
        noise = np.random.default_rng([zlib.crc32(name.encode()), seed]).standard_normal(out[name].shape)
        drawn = base * np.exp(spread * noise) if base else spread * noise
        out[name] = __import__('jax').numpy.asarray(drawn.astype(out[name].dtype))
    for name, factor in factors.items():
        out[name] = (out[name] * factor).astype(out[name].dtype)
    return out
```

```python
import numpy as np
import concourse.bass as bass
from concourse import mybir
from contextlib import ExitStack

F32 = mybir.dt.float32
I32 = mybir.dt.int32
U8 = mybir.dt.uint8
ALU = mybir.AluOpType
ACT = mybir.ActivationFunctionType
AX = mybir.AxisListType

P = 128
D = 1024
KB = D // P
SEQ = 1024
DB, DT = 8, 4
NS = DB * DT
TOK = SEQ + NS
HD = 64
AH = 8
AW = AH * HD
BH, BKV = 8, 2
GRP = BH // BKV
SHIFT_W = 3 * AW + 64 + 64 + 128
IN_W = SHIFT_W + BH * HD + 2 * BKV * HD
WIN = 128
NG, EPG = 4, 4
NE = NG * EPG
FF = 512
HP = AH // 2
NT = SEQ // P
W = 1 + SEQ + DB * (DT + 1)
W1 = W - 1
G3 = [(0, 355), (355, 355), (710, 355)]
G3B = [(0, 355), (355, 355), (710, 354)]
NTT = NT + 1
CAP = 160
SLOTS = NE * CAP
ROUNDS = -(-TOK // CAP)
LV = 7
DECAY = float(np.exp(-0.5))
RMS_EPS, LNX_EPS = 1e-6, 64e-5

SRC_BLOCK = [0, 4, 1, 5, 2, 6, 3, 7, 8, 9, 10, 11, 12, 13, 14, 15, 16, 17, 18, 19]
R_, K_ = (lambda hp: 2 * hp), (lambda hp: 2 * hp + 1)
V_, LORA, GD, Q_, KK_, VV_ = (lambda hp: 8 + hp), 12, 13, 14, 18, 19
ORDER = [(12, 13), (1, 3), (0, 2), (8, 9), (5, 7), (4, 6), (10, 11), (18, 19), (14, 15), (16, 17)]
ARENA = 20 * W + KB * W + HP * W1 + 15504

SEMS = """consts vecs_in lora_in shift_in pad_zero x0 x1 sumsq ms_ok std_ok h_ok hT_ps hT_ok vec_ps vec_ok w0 w1 w2 p_ps p_ok
shT_ps shT_ok prev_ok dve mixed lora_act lora_ps gates_ok kk_sq kk_ps kk_ms kk_std bonus_in bonus_ps exps scaled
blk_done tails_ok ptail_ps ptail_ok sh_out win_out ptail_out smp_in smp_ps smp_ok cum_ok
kvs_ok cache_in bias_in level_in level_ok sc_ps sc_ok m_ok e_ok p_norm pt_ps pt_ok ob_ps ob_ok gam_ok gamma_ok
d_t d_t_act d_t_dve d_eye d_lb d_lb_ok d_lk d_lk_ok d_lc d_lc_ok d_u d_u_ok d_x d_x_ok d_xt d_xt_ok d_g d_g_ok d_m d_m_ok
d_re d_re_ok d_a d_a_ok d_s d_s_ok d_y d_y_ok sf_ps sf_ok
sa_pe sa_act sa_dve r_dve r_act r_pe
sv_out sv_in st_in pool sr_ok sy_out sy_in st_out ys_ps ys_ok
eps_ok f_mean f_yc f_sq f_var f_std f_gate f_mx wo_in x2_in g_in g_ps g_x2 g_lg lg_ok
h2o0 h2o1 hot hot_ps i_ps i_ok n_rounds
xa_ps xa_ok xb_ps xb_ok gu_ps sl_ok ac_ok ya_ps yo_act yo_dve yst0 yst1 round_done rows_done passed pos_ok dve_r xg0 xg1
c0 c1 fin """


def constants():
    i = np.arange(P)
    ident = np.eye(P)
    head_ones = (i[:, None] // HD == i[None, :] // HD) * 1.0
    strict = (i[:, None] < i[None, :]) * 1.0
    upto = (i[:, None] <= i[None, :]) * 1.0
    eye64 = np.tile(np.eye(HD), (2, 1))
    ones = np.ones((P, P))
    iota = np.tile(np.arange(CAP), (P, 1))
    tile_ = np.arange(NT + 1)
    tokid = i[:, None] + P * tile_[None, :]
    table = np.concatenate([ident, head_ones, head_ones / HD, strict, upto, eye64, ones, iota, tokid, tokid < TOK], axis=1)
    levels = []
    for lv in range(LV):
        m = 1 << lv
        low = (i[:, None] // (2 * m) == i[None, :] // (2 * m)) & (i[:, None] % (2 * m) >= m) & (i[None, :] % (2 * m) < m)
        levels += [low, low.T]
    level = np.concatenate(levels, axis=1).astype(np.float32)
    slopes = 2.0 ** (-8.0 * np.arange(1, BH + 1) / BH)
    j = np.arange(2 * P)
    dist = i[:, None] + P - j[None, :]
    ok = (dist >= 0) & (dist < WIN)
    bias = np.stack([np.where(ok, -s * dist, -1e30) for s in slopes], axis=1)
    g, b, t = i // NS, i % NS // DT, i % DT
    j = np.arange(WIN)
    dist = t[:, None] + WIN - j[None, :]
    old = np.where(dist < WIN, dist, -1)
    jb, jt = np.arange(NS) // DT, np.arange(NS) % DT
    new = np.where((b[:, None] == jb) & (jt[None, :] <= t[:, None]), t[:, None] - jt[None, :], -1)
    dist = np.concatenate([old, new], axis=1)
    sbias = np.stack([np.where(dist >= 0, -slopes[kv * GRP + g][:, None] * dist, -1e30) for kv in range(BKV)], axis=1)
    return {"c_table": table.astype(np.float32), "c_level": level, "c_bias": bias.astype(np.float32),
            "c_sbias": sbias.astype(np.float32)}


TABLE = ["ident", "head_ones", "head_mean", "strict", "upto", "eye64", "ones", "iota", "tokid", "valid"]
TABLE_W = dict(ident=P, head_ones=P, head_mean=P, strict=P, upto=P, eye64=HD, ones=P, iota=CAP, tokid=NT + 1, valid=NT + 1)
VECS = ["norm_mix_g", "mu_shift", "w_decay0", "w_iclr0", "k_k", "k_a", "r_k", "lnx_g", "lnx_b", "attn_norm_g"]
VEC_ROWS = [8, 14, 4, 4, 4, 4, 4, 4, 4, 4]


def program(nc, i, o):
    ctx = ExitStack()
    with ctx:
        def sem(name):
            return ctx.enter_context(nc.semaphore(name))

        def sb(name, shape, dt=F32):
            return ctx.enter_context(nc.sbuf_tensor(name, shape, dt))

        table = sb("table", [P, sum(TABLE_W.values())])
        at, T = 0, {}
        for n in TABLE:
            T[n] = table[:, at:at + TABLE_W[n]]
            at += TABLE_W[n]
        ident = T["ident"]
        level = sb("level", [P, 2 * LV * P], U8)
        vecs = sb("vecs", [P, sum(VEC_ROWS)])
        at, V = 0, {}
        for n, k in zip(VECS, VEC_ROWS):
            V[n] = vecs[:, at:at + k]
            at += k
        omka = sb("omka", [P, HP])
        stat = sb("stat", [P, 64])
        wlora = sb("wlora", [P, AW])
        wgate = sb("wgate", [P, AW])
        gam = sb("gam", [P, 2, HP, NT])
        gamma = sb("gamma", [P, HP, NT])
        shT = sb("shT", [P, 14 * DB])
        tails = sb("tails", [P, 14, 1 + DB])

        arena = sb("arena", [P, ARENA])

        def part(at, n):
            assert at + n <= ARENA, (at, n)
            return arena[:, at:at + n]

        pT = part(0, 20 * W).rearrange("p (b w) -> p b w", b=20)
        HT0 = 20 * W
        hTf = part(HT0, KB * W)
        hT = hTf.rearrange("p (b w) -> p b w", b=KB)
        vM = part(HT0 + KB * W, HP * W1).rearrange("p (b w) -> p b w", b=HP)
        F0 = HT0 + KB * W + HP * W1
        wr = part(F0, 3 * 2048).rearrange("p (s b c) -> p s b c", s=3, b=KB)
        xt = part(F0 + 6144, 2 * D).rearrange("p (s d) -> p s d", s=2)
        t_ = [part(F0 + n * W1, W1) for n in range(10)]
        sw, sa, sq, rn, kk, cc, pinv, cex, kt, rt = t_
        bb, rk, fac = rn, sq, sa
        sqj = t_[8][:, 0:D]
        vecs_rows = part(F0 + 10 * W1, P)[0:sum(VEC_ROWS), :]
        shin = part(F0 + 10 * W1 + P, SHIFT_W)[0:DB, :]
        shout = part(F0 + 10 * W1, SHIFT_W)[0:1 + DB, :]
        NP5 = DB * (DT + 1)
        smp = part(F0 + 10 * W1 + SHIFT_W, 6 * AW)[0:NP5, :].rearrange("p (a c) -> p a c", a=6)
        lor = pT[:, LORA, 0:W1]
        sgd = pT[:, GD, 0:W1]
        KBT = hTf[:, 0:HP * SEQ].rearrange("p (b w) -> p b w", b=HP)
        BV = hTf[:, HP * SEQ:HP * SEQ + HP * W1].rearrange("p (b w) -> p b w", b=HP)
        ZR = pT[:, 0:8, :].rearrange("p (h two) w -> p h (two w)", two=2)[:, :, 0:NT * 2 * P].rearrange("p h (c two t) -> p h c two t", c=NT, two=2)
        NBT = pT[:, 8:12, 0:SEQ]

        abias = part(F0, 2048).rearrange("p (h k) -> p h k", h=BH)
        sc = part(F0 + 2048, 2048).rearrange("p (h k) -> p h k", h=BH)
        pt = part(F0 + 4096, 2048).rearrange("p (h k q) -> p h k q", h=BH, k=2)
        vtok = part(F0 + 6144, 1024).rearrange("p (c d) -> p c d", c=NT)
        kc = part(F0 + 7168, 1024).rearrange("p (b d) -> p b d", b=DB)
        vc = part(F0 + 8192, 1024).rearrange("p (b d) -> p b d", b=DB)
        kcT = part(F0 + 9216, 1024).rearrange("p (b k) -> p b k", b=DB)
        sbias = part(F0 + 10240, 320).rearrange("p (v k) -> p v k", v=2)
        ssc = part(F0 + 10560, 320).rearrange("p (v k) -> p v k", v=2)
        sst0 = part(F0 + 10880, 256)
        sst1 = part(F0 + 11136, 256)[0:NS, :]
        kvnew = part(F0 + 11392, 256)[0:NS, :]
        klast = part(F0 + 11648, 128)
        ast = part(F0 + 11776, 64)
        sinkb = part(F0 + 11840, 8)
        sinks = part(F0 + 11848, 2)
        spk0 = part(F0 + 11856, 256)
        spk1 = part(F0 + 12112, 256)[0:NS, :]
        at = F0
        D_ = {}
        for n, k in (("Vt", 512), ("ZG", 1024), ("Kt", 512), ("Bt", 512), ("LB", 2048), ("LK", 2048), ("TL", 1024), ("TT", 1024),
                     ("U", 1024), ("M", 1024), ("AT", 256), ("Sb", 256), ("Re", 512)):
            D_[n] = part(at, k)
            at += k
        assert at == F0 + 11776
        Vt, Kt, Bt = D_["Vt"], D_["Kt"], D_["Bt"]
        ZG, TL, TT, U, M = (D_[n].rearrange("p (h t) -> p h t", h=AH) for n in ("ZG", "TL", "TT", "U", "M"))
        LB, LK = (D_[n].rearrange("p (h two t) -> p h two t", h=AH, two=2) for n in ("LB", "LK"))
        AT, Sb, Re = (D_[n].rearrange("p (h t) -> p h t", h=HP) for n in ("AT", "Sb", "Re"))
        Sout = D_["M"][0:HD, 0:512]
        sst = part(at, 2048).rearrange("p (v k) -> p v k", v=HD // 2)
        svv = part(at + 2048, DT * 6 * HD).rearrange("p (t a k) -> p t a k", t=DT, a=6)
        stm = part(KK_ * W, 2048).rearrange("p (v k) -> p v k", k=HD)
        ssa = sb("ssa", [P, HD // 2])
        sy = sb("sy", [P, DT, HD // 2])
        levelf = part(F0 + 10 * W1 + SHIFT_W, 2 * LV * P)
        YT = KBT
        kvs = sb("kvs", [P, 2, NS])
        qs = sb("qs", [P, GRP * NS])
        yS = sb("yS", [P, HP, NS])
        sv_dram = nc.dram_tensor("sv_dram", [NP5, 6 * AW], F32).ap()
        sy_dram = nc.dram_tensor("sy_dram", [DB * AH, DT, HD], F32).ap()

        yrow = pT[0:NS, LORA, 0:AW]
        NTT = NT + 1
        MX = part(0, 8 * TOK).rearrange("p (b c) -> p b c", b=8)
        X20 = 8 * W
        X2 = part(X20, NTT * D).rearrange("p (t d) -> p t d", t=NTT)
        wo = part(F0, 8 * D).rearrange("p (b n) -> p b n", b=8)
        g_ = [part(F0 + 8192 + n * W1, W1) for n in range(3)]
        gsq, grs, gms = g_
        assert F0 + 8192 + 3 * W1 <= ARENA
        VM0 = HT0 + KB * W
        osq = part(VM0, 4 * TOK).rearrange("p (b c) -> p b c", b=4)
        h2 = part(VM0, 2 * D).rearrange("p (s d) -> p s d", s=2)
        sqj2 = part(F0 + 8192 + D, D)
        h2T = part(VM0 + 2 * D, 2 * D).rearrange("p (s b t) -> p s b t", s=2, b=KB)
        gffn = part(F0 + 8192, D)
        wr20 = part(F0 + 8192 + 2 * D, KB * 20).rearrange("p (b n) -> p b n", b=KB)
        rbias = part(F0 + 8192 + 2 * D + 160, 20)
        R0 = F0 + 8192 + 2 * D + 180
        rt_ = {}
        for n, k in (("lg", 180), ("ga", 36), ("gb", 36), ("ohg", 36), ("prod", 144), ("leg", 36), ("oh1", 36), ("oh2", 36), ("OH1", 144), ("OH2", 144),
                     ("OHs", 144), ("tot", 144), ("rank", 144), ("cnt", 16), ("ei", 18), ("rk", 18), ("ov", 18), ("pos", 18), ("m", 9), ("gw", 9), ("m1", 9), ("m2", 9),
                     ("den", 9), ("mc", 1), ("nr", 1), ("cmp", 1), ("OHT", 288)):
            rt_[n] = part(R0, k)
            R0 += k
        hot = part(R0, 2 * CAP).rearrange("p (s r) -> p s r", s=2)
        R0 += 2 * CAP
        gfin = part(R0, D)
        R0 += D
        assert R0 + 2 * D <= ARENA, R0
        posi = sb("posi", [P, 2, NTT], I32)
        idxA = sb("idxA", [P, NE], I32)
        idxB = sb("idxB", [P, NE], I32)
        nround = sb("nround", [P, 1], I32)
        wts2 = sb("wts2", [P, 2, NTT])
        wtr = sb("wtr", [P, 2, NTT])
        STEPS = 4 + 2 * NTT
        eps = sb("eps", [P, 2])
        h2_dram = nc.dram_tensor("h2_dram", [TOK, D], F32).ap()
        y_dram = nc.dram_tensor("y_dram", [SLOTS, D], F32).ap()
        E0 = X20 + NTT * D
        ew = part(E0, 2 * 3 * 4096)
        egate = [ew[:, n * 12288:n * 12288 + 4096].rearrange("p (b f) -> p b f", b=KB) for n in range(2)]
        eup = [ew[:, n * 12288 + 4096:n * 12288 + 8192].rearrange("p (b f) -> p b f", b=KB) for n in range(2)]
        edown = [ew[:, n * 12288 + 8192:(n + 1) * 12288].rearrange("p (b d) -> p b d", b=FF // P) for n in range(2)]
        XB = CAP - P
        xgA = part(0, 2 * D).rearrange("p (s d) -> p s d", s=2)
        xgB = part(2 * D, 2 * D).rearrange("p (s d) -> p s d", s=2)[0:XB]
        xgT = part(4 * D, 2 * KB * CAP).rearrange("p (s b c) -> p s b c", s=2, b=KB)
        eact = part(4 * D + 2 * KB * CAP, 2 * 4 * CAP).rearrange("p (s f c) -> p s f c", s=2, f=4)
        assert 4 * D + 2 * KB * CAP + 10 * CAP <= X20
        egl = part(4 * D + 2 * KB * CAP + 8 * CAP, 2 * CAP).rearrange("p (s c) -> p s c", s=2)
        Y0 = E0 + 24576
        eyA = part(Y0, 2 * D).rearrange("p (s d) -> p s d", s=2)
        assert Y0 + 2 * D <= F0 + 8192 + 2 * D + 180
        eyB = part(R0, 2 * D).rearrange("p (s d) -> p s d", s=2)[0:XB]
        cy = part(E0, NTT * 2 * D).rearrange("p (t k d) -> p t k d", t=NTT, k=2)
        y_slots = y_dram.rearrange("(e c) d -> e c d", c=CAP)

        ps = ctx.enter_context(nc.psum_tensor("ps", [P, 8, 512], F32))

        def smp_src(hp):
            return [kk, bb, kt, sw, rt, vM[:, hp, :]]

        s = {n: sem(n) for n in SEMS.split()}

        block = ctx.enter_context(nc.Block())

        def toks(i):
            return P if i < NT else NS

        def cols(ap, i):
            if i < NT:
                return ap[:, :, 1 + i * P:1 + (i + 1) * P]
            return ap[:, :, 1 + SEQ:W].rearrange("p b (q t) -> p b q t", t=DT + 1)[:, :, :, 1:]

        def raw_sample(ap):
            return ap[:, SEQ:W1]

        def alone(eng):
            eng.nop().then_inc(s["passed"], 1)

        @block.sync
        def _(sp):
            sp.dma_start(table[:, :], i["c_table"]).then_inc(s["consts"], 16)
            for t in range(2):
                sp.dma_start(xt[:, t, :], i["x_prompt"][0, t * P:(t + 1) * P, :]).then_inc(s[f"x{t}"], 16)
            at = 0
            for n, k in zip(VECS, VEC_ROWS):
                dst = vecs_rows[at:at + k, :]
                src = i[n]
                if n == "r_k":
                    src = src[0].rearrange("(a b) d -> a (b d)", b=2)
                elif n == "attn_norm_g":
                    src = src[0].rearrange("(kv g d) -> g kv d", kv=2, g=GRP)
                    dst = dst.rearrange("g (kv d) -> g kv d", kv=2)
                else:
                    src = src[0].rearrange("(a b) -> a b", b=P)
                sp.dma_start(dst, src).then_inc(s["vecs_in"], 16)
                at += k

            def load_w(u):
                if u >= 3:
                    sp.wait_ge(s["p_ps"], 2 * (u - 2))
                for j, pos in enumerate(ORDER[u]):
                    dst = wr[:, u % 3, :, j * P:(j + 1) * P]
                    src = i["w_in"][0].rearrange("(b p) c -> p b c", p=P)
                    if Q_ <= pos < Q_ + GRP:
                        g = pos - Q_
                        for kv in range(BKV):
                            c = SHIFT_W + HD * (kv * GRP + g)
                            sp.dma_start(dst[:, :, kv * HD:(kv + 1) * HD], src[:, :, c:c + HD]).then_inc(s[f"w{u % 3}"], 16)
                    else:
                        c = SRC_BLOCK[pos] * P
                        sp.dma_start(dst, src[:, :, c:c + P]).then_inc(s[f"w{u % 3}"], 16)

            for t in range(2, NT + 1):
                sp.wait_ge(s["hT_ps"], 2 * (t - 1))
                src = i["x_prompt"][0, t * P:(t + 1) * P, :] if t < NT else i["x_sample"].rearrange("b t d -> (b t) d")
                sp.dma_start(xt[0:toks(t), t % 2, :], src).then_inc(s[f"x{t % 2}"], 16)
                if t in (3, 5, 7):
                    load_w((t - 3) // 2)
            sp.dma_start(shin[:, :], i["state_shift"][0]).then_inc(s["shift_in"], 16)
            sp.dma_start(wlora[0:HD, :], i["w_decay_up"][0]).then_inc(s["lora_in"], 16)
            sp.dma_start(wlora[HD:P, :], i["w_iclr_up"][0]).then_inc(s["lora_in"], 16)
            sp.dma_start(wgate[:, :], i["w_gate_up"][0]).then_inc(s["lora_in"], 16)
            for u in range(3, len(ORDER)):
                load_w(u)
            sp.wait_ge(s["ptail_ok"], 4)
            sp.dma_start(o["state_shift_prompt"][0], shout[0:1, :]).then_inc(s["sh_out"], 16)
            sp.dma_start(o["state_shift_sample"][0], shout[1:1 + DB, :]).then_inc(s["sh_out"], 16)
            sp.wait_ge(s["blk_done"], HP)
            sp.wait_ge(s["scaled"], 2 * HP)
            sp.wait_ge(s["smp_ps"], 2 * HP)
            sp.wait_ge(s["sh_out"], 32)
            sp.wait_ge(s["smp_ok"], 2 * HP)
            sp.dma_start(sv_dram, smp.rearrange("p a c -> p (a c)")).then_inc(s["sv_out"], 16)
            for dst, src in ((kc, "cache_win_k"), (vc, "cache_win_v")):
                sp.dma_start(dst, i[src][0].rearrange("b k v d -> k b (v d)")).then_inc(s["cache_in"], 16)
            sp.dma_start(abias, i["c_bias"]).then_inc(s["bias_in"], 16)
            sp.dma_start(sbias, i["c_sbias"]).then_inc(s["bias_in"], 16)
            sink = i["attn_sink"][0]
            sp.dma_start(sinkb, i["attn_sink"].to_broadcast([P, BH])).then_inc(s["bias_in"], 16)
            for kv in range(BKV):
                sp.dma_start(sinks[:, kv:kv + 1], sink[kv * GRP:(kv + 1) * GRP][:, None, None].to_broadcast([GRP, NS, 1])).then_inc(s["bias_in"], 16)
            sp.wait_ge(s["sa_act"], 1)
            sp.dma_start(o["cache_win_k_prompt"][0, 0].rearrange("t v d -> t (v d)"), klast).then_inc(s["win_out"], 16)
            sp.dma_start(o["cache_win_v_prompt"][0, 0].rearrange("t v d -> t (v d)"), vtok[:, NT - 1, :]).then_inc(s["win_out"], 16)
            for n, (dst, src) in enumerate((("cache_win_k_sample", "cache_win_k"), ("cache_win_v_sample", "cache_win_v"))):
                flat = lambda ap: ap[0].rearrange("b t v d -> b t (v d)")
                sp.dma_start(flat(o[dst])[:, 0:WIN - DT, :], flat(i[src])[:, DT:, :]).then_inc(s["win_out"], 16)
                sp.dma_start(flat(o[dst])[:, WIN - DT:, :], kvnew[:, n * P:(n + 1) * P]).then_inc(s["win_out"], 16)
            sp.wait_ge(s["sv_out"], 16)
            sp.dma_start(levelf, i["c_level"]).then_inc(s["level_in"], 16)
            sp.wait_ge(s["level_ok"], 1)
            for vh in range(2):
                for b in range(DB):
                    q = vh * DB * AH + b * AH
                    sp.dma_start(svv[q:q + AH].rearrange("p t a k -> p (t a) k"),
                                 sv_dram[b * (DT + 1) + 1:(b + 1) * (DT + 1), :].rearrange("t (a h k) -> h (t a) k", a=6, h=AH)).then_inc(s["sv_in"], 16)
            sp.wait_ge(s["ob_ok"], NT)
            sp.wait_ge(s["win_out"], 16 * 6)
            states = lambda ap, vh: ap[0].rearrange("b h v k -> (b h) v k")[:, vh * (HD // 2):(vh + 1) * (HD // 2), :]
            for vh in range(2):
                sp.dma_start(sst[vh * HD:(vh + 1) * HD], states(i["state_rwkv"], vh)).then_inc(s["st_in"], 16)
            sp.wait_ge(s["sr_ok"], 1)
            for vh in range(2):
                sp.dma_start(states(o["state_rwkv_sample"], vh), sst[vh * HD:(vh + 1) * HD]).then_inc(s["st_out"], 16)
                sp.dma_start(sy_dram[:, :, vh * (HD // 2):(vh + 1) * (HD // 2)], sy[vh * HD:(vh + 1) * HD]).then_inc(s["sy_out"], 16)
            sp.wait_ge(s["sy_out"], 32)
            sp.wait_ge(s["pool"], 1)
            for b in range(DB):
                sp.dma_start(yrow[b * DT:(b + 1) * DT, :].rearrange("t (h v) -> t h v", h=AH),
                             sy_dram[b * AH:(b + 1) * AH].rearrange("h t v -> t h v")).then_inc(s["sy_in"], 16)
            sp.wait_ge(s["d_y_ok"], NT)
            sp.wait_ge(s["st_out"], 32)
            sp.dma_start(wo[:, 0:4, :], i["w_out"][0, 0:AW].rearrange("(b p) n -> p b n", p=P)).then_inc(s["wo_in"], 16)
            for kv in range(BKV):
                a = AW + kv * GRP * HD
                sp.dma_start(wo[kv * HD:(kv + 1) * HD, 4:8, :], i["w_out"][0, a:a + GRP * HD].rearrange("(g d) n -> d g n", d=HD)).then_inc(s["wo_in"], 16)
            sp.wait_ge(s["sf_ok"], 1)
            sp.dma_start(o["state_rwkv_prompt"][0, 0].rearrange("h v k -> v h k"), Sout.rearrange("v (h k) -> v h k", h=AH)).then_inc(s["ptail_out"], 16)
            sp.wait_ge(s["ptail_out"], 16)
            sp.wait_ge(s["f_mx"], 2 * GRP + 2 * HP)
            sp.dma_start(X2[:, 0:NT, :], i["x_prompt"][0].rearrange("(t p) d -> p t d", p=P)).then_inc(s["x2_in"], 16)
            sp.dma_start(X2[0:NS, NT, :], i["x_sample"].rearrange("b t d -> (b t) d")).then_inc(s["x2_in"], 16)
            sp.dma_start(gffn, i["norm_ffn_g"].to_broadcast([P, D])).then_inc(s["g_in"], 16)
            sp.dma_start(gfin, i["norm_final_g"][None, :].to_broadcast([P, D])).then_inc(s["g_in"], 16)
            sp.dma_start(wr20[:, :, 0:NG], i["w_route_group"][0].rearrange("(b p) n -> p b n", p=P)).then_inc(s["g_in"], 16)
            sp.dma_start(wr20[:, :, NG:NG + NE], i["w_route_expert"][0].rearrange("(b p) n -> p b n", p=P)).then_inc(s["g_in"], 16)
            sp.dma_start(rbias[:, 0:NG], i["b_route_group"].to_broadcast([P, NG])).then_inc(s["g_in"], 16)
            sp.dma_start(rbias[:, NG:NG + NE], i["b_route_expert"].to_broadcast([P, NE])).then_inc(s["g_in"], 16)
            for t in range(NTT):
                sp.wait_ge(s["h_ok"], NTT + t + 1)
                sp.dma_start(h2_dram[t * P:t * P + toks(t), :], h2[0:toks(t), t % 2, :]).then_inc(s[f"h2o{t % 2}"], 16)
            def load_expert(e, a):
                for dst, name in ((egate, "w_exp_gate"), (eup, "w_exp_up"), (edown, "w_exp_down")):
                    sp.dma_start(dst[a], i[name][0, e].rearrange("(b p) f -> p b f", p=P)).then_inc(s[f"w{a}"], 16)

            sp.wait_ge(s["g_lg"], NTT)
            sp.wait_ge(s["hT_ps"], 4 * NTT)
            sp.wait_ge(s["h_ok"], 2 * NTT)
            sp.wait_ge(s["h2o0"], 16 * 5)
            sp.wait_ge(s["h2o1"], 16 * 4)
            for a in range(2):
                load_expert(a, a)
            sp.wait_ge(s["n_rounds"], 1)
            rounds = sp.value_load(nround[0:1, 0:1], min_val=1, max_val=ROUNDS)
            with sp.Fori(0, ROUNDS) as r:
                with sp.If(rounds > r):
                    with sp.If(r > 0):
                        for a in range(2):
                            load_expert(a, a)
                    with sp.Fori(1, NE // 2) as q:
                        for a in range(2):
                            sp.wait_ge(s["ya_ps"], 4 * (NE * r + 2 * q + a) - 4)
                            load_expert(2 * q + a, a)
                    sp.wait_ge(s["round_done"], r + 1)
                    alone(sp)
            for t in range(NTT):
                sp.wait_ge(s["fin"], t + 1)
                dst = o["y_prompt"][0, t * P:(t + 1) * P, :] if t < NT else o["y_sample"].rearrange("b t d -> (b t) d")
                sp.dma_start(dst, cy[0:toks(t), t, 0, :]).then_inc(s[f"h2o{t % 2}"], 16)
            sp.wait_ge(s["h2o0"], 2 * 16 * 5)
            sp.wait_ge(s["h2o1"], 2 * 16 * 4)
            sp.wait_ge(s["win_out"], 16 * 6)
            sp.wait_ge(s["sh_out"], 32)
            sp.wait_ge(s["st_out"], 32)

        def w_total(u):
            return sum(32 if Q_ <= pos < Q_ + GRP else 16 for v in range(u % 3, u + 1, 3) for pos in ORDER[v])

        PSLOT = {pos: n for n, pos in enumerate(p for pair in ORDER for p in pair)}

        G512 = [(0, 512), (512, 512), (1024, NS)]

        def y_of(hp, n):
            return YT[:, hp, n * 512:(n + 1) * 512] if n < 2 else yS[:, hp, :]

        def sample4(ap):
            return ap.rearrange("p (b t) -> p b t", t=DT + 1)[:, :, 1:]

        def by4(ap):
            return ap.rearrange("p (b t) -> p b t", t=DT)

        WBASE = [w_total(9), w_total(7)]

        @block.tensor
        def _(pe):
            pe.wait_ge(s["consts"], 16)
            pe.wait_ge(s["vecs_in"], 16 * len(VECS))
            nv = sum(VEC_ROWS)
            pe.transpose(ps[:, 7, 0:nv], vecs_rows[:, :], ident[0:nv, 0:nv]).then_inc(s["vec_ps"], 1)
            for t in range(NT + 1):
                pe.wait_ge(s["h_ok"], t + 1)
                n = toks(t)
                for j in range(2):
                    if t >= 2:
                        pe.wait_ge(s["hT_ok"], 2 * (t - 2) + j + 1)
                    for k in range(4):
                        last = pe.transpose(ps[:, 2 * (t % 2) + j, k * n:(k + 1) * n], xt[0:n, t % 2, (4 * j + k) * P:(4 * j + k + 1) * P],
                                            ident[0:n, 0:n])
                    last.then_inc(s["hT_ps"], 1)
            pe.wait_ge(s["shift_in"], 16)
            for c in range(14):
                last = pe.transpose(ps[:, 7, P + c * DB:P + (c + 1) * DB], shin[:, c * P:(c + 1) * P], ident[0:DB, 0:DB])
            last.then_inc(s["shT_ps"], 1)
            pe.wait_ge(s["hT_ok"], 2 * (NT + 1))
            pe.wait_ge(s["pad_zero"], 1)
            for u, pair in enumerate(ORDER):
                pe.wait_ge(s[f"w{u % 3}"], w_total(u))
                for j in range(2):
                    n = 2 * u + j
                    if n >= 2:
                        pe.wait_ge(s["p_ok"], n - 1)
                    for k in range(KB):
                        for g, (a, m) in enumerate(G3):
                            last = pe.matmul(ps[:, 3 * (n % 2) + g, 0:m], wr[:, u % 3, k, j * P:(j + 1) * P], hT[:, k, a:a + m],
                                             start=(k == 0), stop=(k == KB - 1))
                    last.then_inc(s["p_ps"], 1)
            pe.wait_ge(s["tails_ok"], 4)
            for q in range(4):
                if q >= 2:
                    pe.wait_ge(s["ptail_ok"], q - 1)
                for c in range(4 * q, min(4 * q + 4, 14)):
                    last = pe.transpose(ps[0:1 + DB, 6 + q % 2, (c % 4) * P:(c % 4 + 1) * P], tails[:, SRC_BLOCK.index(c), :], ident)
                last.then_inc(s["ptail_ps"], 1)
            pe.wait_ge(s["lora_in"], 48)
            for hp in range(HP):
                c = slice(hp * P, (hp + 1) * P)
                if hp == 0:
                    pe.wait_ge(s["lora_act"], 2)
                if hp >= 1:
                    pe.wait_ge(s["blk_done"], hp)
                    pe.wait_ge(s["kk_ms"], hp)
                for g, (a, m) in enumerate(G3B):
                    pe.matmul(ps[:, g, 0:m], wlora[0:HD, c], lor[0:HD, a:a + m], start=True, stop=True)
                for g, (a, m) in enumerate(G3B):
                    last = pe.matmul(ps[:, 3 + g, 0:m], wlora[HD:P, c], lor[HD:P, a:a + m], start=True, stop=True)
                last.then_inc(s["lora_ps"], 1)
                pe.wait_ge(s["kk_sq"], hp + 1)
                pe.wait_ge(s["gates_ok"], 2 * hp + 2)
                for g, (a, m) in enumerate(G3B):
                    last = pe.matmul(ps[:, g, 0:m], T["head_ones"], sq[:, a:a + m], start=True, stop=True)
                last.then_inc(s["kk_ps"], 1)
                pe.wait_ge(s["bonus_in"], hp + 1)
                for g, (a, m) in enumerate(G3B):
                    last = pe.matmul(ps[:, 3 + g, 0:m], T["head_ones"], rk[:, a:a + m], start=True, stop=True)
                last.then_inc(s["bonus_ps"], 1)
                pe.wait_ge(s["smp_in"], hp + 1)
                if hp >= 1:
                    pe.wait_ge(s["smp_ok"], 2 * hp)
                for n, ap in enumerate(smp_src(hp)):
                    last = pe.transpose(ps[0:NP5, 6 + n // 3, (n % 3) * P:(n % 3 + 1) * P], raw_sample(ap), ident)
                    if n % 3 == 2:
                        last.then_inc(s["smp_ps"], 1)

            def q_of(g, kv, t):
                return pT[kv * HD:(kv + 1) * HD, Q_ + g, 1 + t * P:1 + (t + 1) * P]

            pe.wait_ge(s["smp_ok"], 2 * HP)
            pe.wait_ge(s["blk_done"], HP)
            pe.wait_ge(s["kvs_ok"], 1)
            for c in range(NT):
                last = pe.transpose(ps[:, c // 4, c % 4 * P:(c % 4 + 1) * P], pT[:, VV_, 1 + c * P:1 + (c + 1) * P], ident)
            pe.transpose(ps[:, 2, 0:P], pT[:, KK_, 1 + SEQ - P:1 + SEQ], ident)
            for n, pos in enumerate((KK_, VV_)):
                last = pe.transpose(ps[0:NS, 2, (n + 1) * P:(n + 2) * P], kvs[:, n, :], ident)
            last.then_inc(s["sa_pe"], 1)
            pe.wait_ge(s["cache_in"], 32)
            for b in range(DB):
                last = pe.transpose(ps[:, 4 + b // 4, b % 4 * P:(b % 4 + 1) * P], kc[:, b, :], ident)
            last.then_inc(s["sa_pe"], 1)
            pe.wait_ge(s["sa_act"], 1)
            pe.wait_ge(s["sa_act"], 2)
            for kv in range(BKV):
                r = slice(kv * HD, (kv + 1) * HD)
                for b in range(DB):
                    c = 1 + SEQ + b * (DT + 1) + 1
                    out = ps[:, 6 + kv, 0:P].rearrange("p (g b t) -> p g b t", g=GRP, b=DB)[:, :, b, :]
                    pe.matmul(out, kcT[r, b, :], pT[r, Q_:Q_ + GRP, c:c + DT], start=True, stop=True)
            for kv in range(BKV):
                r = slice(kv * HD, (kv + 1) * HD)
                last = pe.matmul(ps[0:NS, 4 + kv, 0:P], kvs[r, 0, :], qs[r, :], start=True, stop=True)
            last.then_inc(s["sa_pe"], 1)
            pe.wait_ge(s["sa_act"], 4)
            for kv in range(BKV):
                pe.transpose(ps[:, 6, kv * 160:kv * 160 + P], sst0[:, kv * P:(kv + 1) * P], ident)
                last = pe.transpose(ps[:, 6, kv * 160 + P:(kv + 1) * 160], sst1[:, kv * P:(kv + 1) * P], ident[0:NS, 0:NS])
            last.then_inc(s["sa_pe"], 1)
            pe.wait_ge(s["sa_dve"], 2)
            for kv in range(BKV):
                pe.transpose(ps[:, 6, kv * P:(kv + 1) * P], ssc[:, kv, 0:P], ident)
                last = pe.transpose(ps[0:NS, 7, kv * P:(kv + 1) * P], ssc[:, kv, P:160], ident)
            last.then_inc(s["sa_pe"], 1)
            pe.wait_ge(s["sa_act"], 7)
            for kv in range(BKV):
                r = slice(kv * HD, (kv + 1) * HD)
                out = ps[r, 6, 0:P]
                pe.matmul(out, kvnew[:, P + kv * HD:P + (kv + 1) * HD], spk1[:, kv * P:(kv + 1) * P], start=True, stop=False, skip_group_check=True)
                for b in range(DB):
                    view = lambda ap: ap.rearrange("p (g b t) -> p g b t", g=GRP, b=DB)[:, :, b, :]
                    last = pe.matmul(view(out), vc[:, b, r], view(spk0[:, kv * P:(kv + 1) * P]), start=False, stop=(b == DB - 1), skip_group_check=True)
            last.then_inc(s["sa_pe"], 1)
            pe.wait_ge(s["sa_act"], 8)
            for t in range(NT):
                nk = 1 if t == 0 else 2
                k0 = max(t - 1, 0) * P
                if t >= 1:
                    pe.wait_ge(s["sc_ok"], t)
                for h in range(BH):
                    kv, g = h // GRP, h % GRP
                    last = pe.matmul(ps[:, h // 2, h % 2 * 256:h % 2 * 256 + nk * P], q_of(g, kv, t),
                                     pT[kv * HD:(kv + 1) * HD, KK_, 1 + k0:1 + k0 + nk * P], start=True, stop=True)
                last.then_inc(s["sc_ps"], 1)
                pe.wait_ge(s["p_norm"], t + 1)
                for r in range(4):
                    if t or r >= 2:
                        pe.wait_ge(s["pt_ok"], 4 * t + r - 1)
                    for h in (2 * r, 2 * r + 1):
                        for k in range(nk):
                            c = (h % 2 * 2 + k) * P
                            last = pe.transpose(ps[:, 4 + r % 2, c:c + P], sc[:, h, k * P:(k + 1) * P], ident)
                    last.then_inc(s["pt_ps"], 1)
                if t >= 1:
                    pe.wait_ge(s["ob_ok"], t)
                for h in range(BH):
                    kv, g = h // GRP, h % GRP
                    pe.wait_ge(s["pt_ok"], 4 * t + h // 2 + 1)
                    for k in range(nk):
                        last = pe.matmul(ps[kv * HD:(kv + 1) * HD, 6, g * P:(g + 1) * P], vtok[:, k0 // P + k, kv * HD:(kv + 1) * HD],
                                         pt[:, h, k, :], start=(k == 0), stop=(k == nk - 1))
                last.then_inc(s["ob_ps"], 1)

            def row(h):
                return slice(h % 2 * HD, (h % 2 + 1) * HD)

            for c in range(NT):
                ct = slice(c * P, (c + 1) * P)
                if c == 0:
                    pe.wait_ge(s["scaled"], 2 * HP)
                    pe.wait_ge(s["sc_ok"], NT)
                else:
                    pe.wait_ge(s["d_m_ok"], 2 * c)
                    pe.wait_ge(s["d_re_ok"], c)
                    pe.wait_ge(s["d_a_ok"], c)
                for n, src in enumerate((vM[:, :, ct], ZR[:, :, c, 0, :], KBT[:, :, ct], NBT[:, :, ct])):
                    for hp in range(HP):
                        last = pe.transpose(ps[:, n, hp * P:(hp + 1) * P], src[:, hp, :], ident)
                    last.then_inc(s["d_t"], 1)
                if c == 0:
                    pe.wait_ge(s["ob_ok"], NT)
                else:
                    pe.wait_ge(s["d_s_ok"], c)
                    pe.wait_ge(s["d_y_ok"], c)
                for hf in range(2):
                    for n, L in enumerate((NBT, KBT)):
                        if hf:
                            pe.wait_ge(s[("d_lb_ok", "d_lk_ok")[n]], 2 * c + 1)
                        for h in range(4 * hf, 4 * hf + 4):
                            last = pe.matmul(ps[:, 4 + 2 * n + h % 2, h % 4 // 2 * 256:(h % 4 // 2 + 1) * 256], L[row(h), h // 2, ct],
                                             ZR[row(h), h // 2, c, :, :], start=True, stop=True)
                        last.then_inc(s[("d_lb", "d_lk")[n]], 1)
                pe.wait_ge(s["d_t_act"], 2 * c + 1)
                pe.wait_ge(s["d_t_dve"], 2 * c + 1)
                for h in range(AH):
                    last = pe.matmul(ps[:, h % 2, h // 2 * P:(h // 2 + 1) * P], ZR[row(h), h // 2, c, 0, :], NBT[row(h), h // 2, ct],
                                     start=True, stop=True)
                last.then_inc(s["d_lc"], 1)
                for lv in range(1, LV):
                    for hf in range(2):
                        n = 2 * ((LV - 1) * c + lv - 1) + hf
                        if lv == 1:
                            pe.wait_ge(s["d_lc_ok"], 4 * (c + 1))
                            pe.wait_ge(s["d_lb_ok"], 2 * c + hf + 1)
                        else:
                            pe.wait_ge(s["d_x_ok"], n - 1)
                        for h in range(4 * hf, 4 * hf + 4):
                            last = pe.matmul(ps[:, hf, h % 4 * P:(h % 4 + 1) * P], LB[:, h, 0, :], TL[:, h, :], start=True, stop=True)
                        last.then_inc(s["d_u"], 1)
                    for hf in range(2):
                        n = 2 * ((LV - 1) * c + lv - 1) + hf
                        pe.wait_ge(s["d_u_ok"], n + 1)
                        if lv == 1 and hf == 0:
                            pe.wait_ge(s["d_t_act"], 2 * c + 2)
                        if lv == 1 and hf == 1:
                            pe.wait_ge(s["d_t_dve"], 2 * c + 2)
                        if lv > 1:
                            pe.wait_ge(s["d_xt_ok"], n - 1)
                        else:
                            pe.wait_ge(s["d_lb_ok"], 2 * c + 2)
                        for h in range(4 * hf, 4 * hf + 4):
                            last = pe.matmul(ps[:, 2 + hf, h % 4 * P:(h % 4 + 1) * P], TT[:, h, :], U[:, h, :], start=True, stop=True)
                        last.then_inc(s["d_x"], 1)
                        for h in range(4 * hf, 4 * hf + 4):
                            last = pe.matmul(ps[:, 4 + hf, h % 4 * P:(h % 4 + 1) * P], U[:, h, :], TT[:, h, :], start=True, stop=True)
                        last.then_inc(s["d_xt"], 1)
                pe.wait_ge(s["d_lk_ok"], 2 * c + 2)
                for h in range(AH):
                    last = pe.matmul(ps[:, 6, h * HD:(h + 1) * HD], LK[:, h, 0, :], Vt[:, h * HD:(h + 1) * HD], start=True, stop=True)
                last.then_inc(s["d_g"], 1)
                pe.wait_ge(s["d_g_ok"], c + 1)
                pe.wait_ge(s["d_xt_ok"], 2 * (LV - 1) * (c + 1))
                pe.wait_ge(s["d_u_ok"], 2 * (LV - 1) * (c + 1))
                for hf in range(2):
                    for h in range(4 * hf, 4 * hf + 4):
                        last = pe.matmul(ps[:, hf, h % 4 * P:(h % 4 + 1) * P], TT[:, h, :], ZG[:, h, :], start=True, stop=True)
                    last.then_inc(s["d_m"], 1)
                pe.wait_ge(s["d_m_ok"], 2 * c + 2)
                pe.wait_ge(s["d_x_ok"], 2 * (LV - 1) * (c + 1))
                for h in range(AH):
                    last = pe.matmul(ps[row(h), 2, h // 2 * P:(h // 2 + 1) * P], M[:, h, 0:HD], LB[:, h, 1, :], start=True, stop=True)
                last.then_inc(s["d_re"], 1)
                for h in range(AH):
                    last = pe.matmul(ps[row(h), 3, h // 2 * HD:(h // 2 + 1) * HD], M[:, h, 0:HD], Bt[:, h * HD:(h + 1) * HD], start=True, stop=True)
                last.then_inc(s["d_a"], 1)
                for h in range(AH):
                    pe.matmul(ps[row(h), 4, h // 2 * HD:(h // 2 + 1) * HD], Kt[:, h * HD:(h + 1) * HD], Vt[:, h * HD:(h + 1) * HD],
                              start=(h < 2), stop=False, skip_group_check=True)
                    last = pe.matmul(ps[row(h), 4, h // 2 * HD:(h // 2 + 1) * HD], Bt[:, h * HD:(h + 1) * HD], M[:, h, HD:],
                                     start=False, stop=(c == 0), skip_group_check=True)
                if c == 0:
                    last.then_inc(s["d_s"], 1)
                for h in range(AH):
                    pe.matmul(ps[row(h), 5, h // 2 * P:(h // 2 + 1) * P], Vt[:, h * HD:(h + 1) * HD], LK[:, h, 1, :],
                              start=(h < 2), stop=False, skip_group_check=True)
                    last = pe.matmul(ps[row(h), 5, h // 2 * P:(h // 2 + 1) * P], M[:, h, HD:], LB[:, h, 1, :],
                                     start=False, stop=(c == 0), skip_group_check=True)
                if c == 0:
                    last.then_inc(s["d_y"], 1)
                else:
                    pe.wait_ge(s["d_s_ok"], c)
                    pe.wait_ge(s["d_a_ok"], c + 1)
                    for h in range(AH):
                        last = pe.matmul(ps[row(h), 4, h // 2 * HD:(h // 2 + 1) * HD], AT[row(h), h // 2, :], Sb[row(h), h // 2, :],
                                         start=False, stop=True, skip_group_check=True)
                    last.then_inc(s["d_s"], 1)
                    pe.wait_ge(s["d_re_ok"], c + 1)
                    for h in range(AH):
                        last = pe.matmul(ps[row(h), 5, h // 2 * P:(h // 2 + 1) * P], Sb[row(h), h // 2, :], Re[row(h), h // 2, :],
                                         start=False, stop=True, skip_group_check=True)
                    last.then_inc(s["d_y"], 1)
            pe.wait_ge(s["d_s_ok"], NT)
            for hp in range(HP):
                last = pe.transpose(ps[0:HD, 6, hp * P:(hp + 1) * P], Sb[:, hp, :], ident)
            last.then_inc(s["sf_ps"], 1)

            pe.wait_ge(s["f_sq"], 1)
            pe.wait_ge(s["d_y_ok"], NT)
            for n, (a, m) in enumerate(G512):
                for g in range(GRP):
                    last = pe.matmul(ps[:, 3 + n, 0:m], T["ones"], osq[:, g, a:a + m], start=(g == 0), stop=(g == GRP - 1))
            last.then_inc(s["f_var"], 1)
            pe.wait_ge(s["sy_in"], 16 * DB)
            pe.wait_ge(s["sf_ok"], 1)
            for hp in range(HP):
                last = pe.transpose(ps[:, 6, hp * NS:(hp + 1) * NS], yrow[:, hp * P:(hp + 1) * P], ident[0:NS, 0:NS])
            last.then_inc(s["ys_ps"], 1)
            pe.wait_ge(s["ys_ok"], 1)
            for hp in range(HP):
                if hp >= 1:
                    pe.wait_ge(s["f_yc"], hp)
                for n, (a, m) in enumerate(G512):
                    last = pe.matmul(ps[:, n, 0:m], T["head_mean"], y_of(hp, n), start=True, stop=True)
                last.then_inc(s["f_mean"], 1)
                pe.wait_ge(s["f_sq"], 1 + hp + 1)
                if hp == 0:
                    pe.wait_ge(s["f_std"], 1)
                else:
                    pe.wait_ge(s["f_std"], 1 + hp)
                for n, (a, m) in enumerate(G512):
                    last = pe.matmul(ps[:, 3 + n, 0:m], T["head_mean"], gsq[:, a:a + m], start=True, stop=True)
                last.then_inc(s["f_var"], 1)
                if hp >= 1:
                    pe.wait_ge(s["f_mx"], 2 * GRP + 2 * hp)
                pe.wait_ge(s["f_yc"], hp + 1)
                c = slice(hp * P, (hp + 1) * P)
                pe.matmul(ps[:, 6, :], wgate[:, c], sgd[:, 0:512], start=True, stop=True)
                pe.matmul(ps[:, 7, :], wgate[:, c], sgd[:, 512:1024], start=True, stop=True)
                pe.wait_ge(s["f_std"], 1 + hp + 1)
                pe.matmul(ps[:, 5, NS:2 * NS], wgate[:, c], sgd[:, SEQ:W1].rearrange("p (b t) -> p b t", t=DT + 1)[:, :, 1:],
                          start=True, stop=True).then_inc(s["f_gate"], 1)

            def project(t):
                n = toks(t)
                if t >= 2:
                    pe.wait_ge(s["g_x2"], t - 1)
                for hf in range(2):
                    for b in range(8):
                        last = pe.matmul(ps[0:n, 2 * (t % 2) + hf, :], MX[:, b, t * P:t * P + n], wo[:, b, hf * 512:(hf + 1) * 512],
                                         start=(b == 0), stop=(b == 7))
                last.then_inc(s["g_ps"], 1)

            pe.wait_ge(s["f_mx"], 2 * GRP + 2 * HP)
            pe.wait_ge(s["wo_in"], 48)
            project(0)
            for t in range(NTT):
                n = toks(t)
                if t + 1 < NTT:
                    project(t + 1)
                pe.wait_ge(s["h_ok"], NTT + t + 1)
                for j in range(2):
                    if t >= 1:
                        pe.wait_ge(s["hT_ok"], 2 * NTT + 2 * (t - 1) + j + 1)
                    for k in range(4):
                        last = pe.transpose(ps[:, 4 + j, k * n:(k + 1) * n], h2[0:n, t % 2, (4 * j + k) * P:(4 * j + k + 1) * P], ident[0:n, 0:n])
                    last.then_inc(s["hT_ps"], 1)
                pe.wait_ge(s["hT_ok"], 2 * NTT + 2 * t + 2)
                if t == 0:
                    pe.wait_ge(s["g_in"], 16 * 6)
                for k in range(KB):
                    last = pe.matmul(ps[0:n, 6, t * 20:(t + 1) * 20], h2T[:, t % 2, k, 0:n], wr20[:, k, :], start=(k == 0), stop=(k == KB - 1))
                last.then_inc(s["g_lg"], 1)
            pe.wait_ge(s["r_dve"], 3)
            pe.matmul(ps[:, 7, 0:NTT * NE], T["strict"], rt_["OHs"], start=True, stop=True)
            pe.matmul(ps[:, 7, NTT * NE:2 * NTT * NE], T["ones"], rt_["OHs"], start=True, stop=True).then_inc(s["r_pe"], 1)

            def turn(g, a, first):
                pe.wait_ge(s[f"xg{a}"], 16 * g + (32 - 16 * a))
                for j in range(2):
                    if not first:
                        pe.wait_ge(s["xa_ok"], 2 * g + (j - 1))
                    for k in range(4):
                        last = pe.transpose(ps[:, j, k * P:(k + 1) * P], xgA[:, a, (4 * j + k) * P:(4 * j + k + 1) * P], ident)
                    last.then_inc(s["xa_ps"], 1)
                if not first:
                    pe.wait_ge(s["xb_ok"], g)
                    alone(pe)
                for k in range(KB):
                    last = pe.transpose(ps[:, 2, k * XB:(k + 1) * XB], xgB[:, a, k * P:(k + 1) * P], ident[0:XB, 0:XB])
                last.then_inc(s["xb_ps"], 1)

            def gate_up(g, a, first):
                pe.wait_ge(s["xa_ok"], 2 * g + 2)
                pe.wait_ge(s["xb_ok"], g + 1)
                pe.wait_ge(s[f"w{a}"], WBASE[a] + 24 * g + (48 - 24 * a))
                for f in range(4):
                    if not (first and f < 2):
                        pe.wait_ge(s["ac_ok"], 4 * g + (f - 1))
                    for n, w in enumerate((egate, eup)):
                        for k in range(KB):
                            last = pe.matmul(ps[:, 3 + f % 2, n * CAP:(n + 1) * CAP], w[a][:, k, f * P:(f + 1) * P], xgT[:, a, k, :],
                                             start=(k == 0), stop=(k == KB - 1))
                    last.then_inc(s["gu_ps"], 1)

            def down(g, a, first):
                pe.wait_ge(s["ac_ok"], 4 * g + 4)
                for n, bank in enumerate((5, 6, 7, 5)):
                    if n == 3:
                        pe.wait_ge(s["yo_act"], 2 * g + 1)
                    elif not first:
                        pe.wait_ge(s[("yo_dve", "yo_dve", "yo_act")[n]], 2 * g)
                    m, at = ((P, 0), (XB, P))[n // 2]
                    for k in range(4):
                        last = pe.matmul(ps[0:m, bank, :], eact[:, a, k, at:at + m], edown[a][:, k, n % 2 * 512:(n % 2 + 1) * 512], start=(k == 0), stop=(k == 3))
                    last.then_inc(s["ya_ps"], 1)

            pe.wait_ge(s["n_rounds"], 1)
            rounds = pe.value_load(nround[0:1, 0:1], min_val=1, max_val=ROUNDS)
            with pe.Fori(0, ROUNDS) as r:
                with pe.If(rounds > r):
                    for m in range(2 * NTT):
                        pe.wait_ge(s["hot"], 2 * NTT * r + m + 1)
                        rhs = rt_["OHT"][:, m * NE:(m + 1) * NE]
                        pe.matmul(ps[:, 7, 0:NE], hot[:, m % 2, 0:P], rhs, start=(m == 0), stop=(m == 2 * NTT - 1))
                        pe.matmul(ps[0:XB, 6, 0:NE], hot[:, m % 2, P:CAP], rhs, start=(m == 0), stop=(m == 2 * NTT - 1)).then_inc(s["hot_ps"], 1)
                    pe.wait_ge(s["i_ok"], r + 1)
                    g0 = NE * r
                    turn(g0, 0, True)
                    gate_up(g0, 0, True)
                    turn(g0 + 1, 1, False)
                    down(g0, 0, True)
                    gate_up(g0 + 1, 1, False)
                    with pe.Fori(1, NE // 2) as q:
                        g = NE * r + 2 * q
                        turn(g, 0, False)
                        down(g - 1, 1, False)
                        gate_up(g, 0, False)
                        turn(g + 1, 1, False)
                        down(g, 0, False)
                        gate_up(g + 1, 1, False)
                    down(g0 + (NE - 1), 1, False)
                    pe.wait_ge(s["round_done"], r + 1)
                    alone(pe)

        @block.scalar
        def _(act):
            act.wait_ge(s["vec_ps"], 1)
            act.copy(vecs[:, :], ps[:, 7, 0:sum(VEC_ROWS)]).then_inc(s["vec_ok"], 1)
            for t in range(NT + 1):
                n = toks(t)
                act.wait_ge(s[f"x{t % 2}"], 16 * (t // 2 + 1))
                act.activation(sqj[0:n, :], xt[0:n, t % 2, :], ACT.Square, accum_out=stat[0:n, t:t + 1]).then_inc(s["sumsq"], 1)
                act.wait_ge(s["ms_ok"], t + 1)
                act.activation(stat[0:n, 20 + t:21 + t], stat[0:n, 10 + t:11 + t], ACT.Sqrt).then_inc(s["std_ok"], 1)
            act.wait_ge(s["shT_ps"], 1)
            act.copy(shT[:, :], ps[:, 7, P:P + 14 * DB]).then_inc(s["shT_ok"], 1)
            act.wait_ge(s["shT_ok"], 1)
            for n in range(20):
                pos = ORDER[n // 2][n % 2]
                act.wait_ge(s["p_ps"], n + 1)
                act.copy(pT[:, pos, :].rearrange("p (g c) -> p g c", g=3), ps[:, 3 * (n % 2):3 * (n % 2) + 3, 0:355]).then_inc(s["p_ok"], 1)
                if pos < 14:
                    act.wait_ge(s["p_ok"], n + 1)
                    c = SRC_BLOCK[pos]
                    act.copy(pT[:, pos, 1 + SEQ:W:DT + 1], shT[:, c * DB:(c + 1) * DB]).then_inc(s["prev_ok"], 1)
                if n == 1:
                    act.wait_ge(s["mixed"], 2)
                    act.activation(lor[0:HD, :], kt[0:HD, :], ACT.Tanh).then_inc(s["lora_act"], 1)
                    act.copy(lor[HD:P, :], kt[HD:P, :]).then_inc(s["lora_act"], 1)
                    act.activation(sgd[:, :], rt[:, :], ACT.Sigmoid).then_inc(s["lora_act"], 1)
            for q in range(4):
                act.wait_ge(s["ptail_ps"], q + 1)
                m = min(4, 14 - 4 * q) * P
                act.copy(shout[:, 4 * q * P:4 * q * P + m], ps[0:1 + DB, 6 + q % 2, 0:m]).then_inc(s["ptail_ok"], 1)
            for hp in range(HP):
                act.wait_ge(s["lora_ps"], hp + 1)
                if hp >= 1:
                    act.wait_ge(s["blk_done"], hp)
                    act.wait_ge(s["scaled"], 2 * hp)
                for g, (dst, bias) in enumerate(((sw, "w_decay0"), (sa, "w_iclr0"))):
                    for n, (a, m) in enumerate(G3B):
                        last = act.activation(dst[:, a:a + m], ps[:, 3 * g + n, 0:m], ACT.Sigmoid, bias=V[bias][:, hp:hp + 1])
                    last.then_inc(s["gates_ok"], 1)
                act.wait_ge(s["mixed"], 2 + 3 * hp + 1)
                act.activation(sq[:, :], kt[:, :], ACT.Square, scale=V["k_k"][:, hp:hp + 1]).then_inc(s["kk_sq"], 1)
                act.wait_ge(s["kk_ms"], hp + 1)
                act.activation(rn[:, :], rn[:, :], ACT.Sqrt).then_inc(s["kk_std"], 1)
                act.wait_ge(s["cum_ok"], hp + 1)
                act.activation(pinv[:, 0:SEQ], cc[:, 0:SEQ], ACT.Exp, scale=DECAY).then_inc(s["exps"], 1)
                act.activation(cex[:, 0:SEQ], cex[:, 0:SEQ], ACT.Exp, scale=-DECAY).then_inc(s["exps"], 1)
                act.activation(cc[:, 0:SEQ], cc[:, 0:SEQ], ACT.Exp, scale=-DECAY).then_inc(s["exps"], 1)
                act.activation(raw_sample(sw), raw_sample(sw), ACT.Exp, scale=-DECAY).then_inc(s["exps"], 1)
                for n in range(2):
                    act.wait_ge(s["smp_ps"], 2 * hp + n + 1)
                    act.copy(smp[:, 3 * n:3 * n + 3, hp * P:(hp + 1) * P], ps[0:NP5, 6 + n, 0:3 * P].rearrange("p (a c) -> p a c", a=3)).then_inc(s["smp_ok"], 1)

            act.wait_ge(s["sa_pe"], 1)
            act.wait_ge(s["scaled"], 2 * HP)
            act.wait_ge(s["sh_out"], 32)
            act.copy(vtok.rearrange("p c d -> p (c d)").rearrange("p (b c) -> p b c", b=2), ps[:, 0:2, :])
            act.copy(klast, ps[:, 2, 0:P])
            act.copy(kvnew, ps[0:NS, 2, P:3 * P]).then_inc(s["sa_act"], 1)
            act.wait_ge(s["sa_pe"], 2)
            act.copy(kcT.rearrange("p b k -> p (b k)").rearrange("p (b c) -> p b c", b=2), ps[:, 4:6, :]).then_inc(s["sa_act"], 1)
            act.wait_ge(s["sa_pe"], 3)
            act.copy(sst0.rearrange("p (v c) -> p v c", v=2), ps[:, 6:8, 0:P]).then_inc(s["sa_act"], 1)
            act.copy(sst1.rearrange("p (v c) -> p v c", v=2), ps[0:NS, 4:6, 0:P]).then_inc(s["sa_act"], 1)
            act.wait_ge(s["sa_dve"], 1)
            for kv in range(BKV):
                act.activation(ssc[:, kv, :], ssc[:, kv, :], ACT.Exp, bias=ast[:, 32 + kv:33 + kv], accum_out=ast[:, 34 + kv:35 + kv])
            act.activation(ast[:, 36:38], ast[:, 38:40], ACT.Exp).then_inc(s["sa_act"], 1)
            act.wait_ge(s["sa_pe"], 5)
            act.copy(spk0, ps[:, 6, 0:2 * P]).then_inc(s["sa_act"], 1)
            act.copy(spk1, ps[0:NS, 7, 0:2 * P]).then_inc(s["sa_act"], 1)
            act.wait_ge(s["sa_pe"], 6)
            for g in range(GRP):
                last = act.copy(pT[:, Q_ + g, 1 + SEQ:W].rearrange("p (b t) -> p b t", t=DT + 1)[:, :, 1:],
                                ps[:, 6, g * NS:(g + 1) * NS].rearrange("p (b t) -> p b t", t=DT))
            last.then_inc(s["sa_act"], 1)
            for t in range(NT):
                nk = 1 if t == 0 else 2
                act.wait_ge(s["m_ok"], t + 1)
                for h in range(BH):
                    act.activation(sc[:, h, 0:nk * P], sc[:, h, 0:nk * P], ACT.Exp, bias=ast[:, h:h + 1], accum_out=ast[:, 8 + h:9 + h])
                act.activation(ast[:, 16:24], ast[:, 24:32], ACT.Exp).then_inc(s["e_ok"], 1)
                for r in range(4):
                    act.wait_ge(s["pt_ps"], 4 * t + r + 1)
                    if t and r == 0:
                        act.wait_ge(s["ob_ps"], t)
                    act.copy(pt[:, 2 * r:2 * r + 2, 0:nk, :], ps[:, 4 + r % 2, :].rearrange("p (h k q) -> p h k q", h=2, k=2)[:, :, 0:nk, :])\
                       .then_inc(s["pt_ok"], 1)
                act.wait_ge(s["ob_ps"], t + 1)
                act.copy(pT[:, Q_:Q_ + GRP, 1 + t * P:1 + (t + 1) * P], ps[:, 6, :].rearrange("p (g q) -> p g q", g=GRP)).then_inc(s["ob_ok"], 1)
            act.wait_ge(s["gam_ok"], 1)
            act.activation(gamma[:, :, :], gam[:, 1, :, :], ACT.Exp, scale=-DECAY).then_inc(s["gamma_ok"], 1)
            act.wait_ge(s["win_out"], 16 * 6)
            for c in range(NT):
                if c >= 1:
                    act.wait_ge(s["d_m"], 2 * c)
                act.wait_ge(s["ob_ps"], NT)
                act.copy(TL, ident[:, None, :].to_broadcast([P, AH, P])).then_inc(s["d_eye"], 1)
                act.copy(TT, ident[:, None, :].to_broadcast([P, AH, P])).then_inc(s["d_eye"], 1)
                act.wait_ge(s["d_t"], 4 * c + 1)
                if c >= 1:
                    act.wait_ge(s["d_y"], c)
                act.copy(Vt, ps[:, 0, :]).then_inc(s["d_t_act"], 1)
                act.wait_ge(s["d_t"], 4 * c + 3)
                act.copy(Kt, ps[:, 2, :]).then_inc(s["d_t_act"], 1)
                for lv in range(1, LV):
                    for hf in range(2):
                        n = 2 * ((LV - 1) * c + lv - 1) + hf
                        act.wait_ge(s["d_u"], n + 1)
                        if n >= 2:
                            act.wait_ge(s["d_xt"], n - 1)
                        act.copy(U[:, 4 * hf:4 * hf + 4, :], ps[:, hf, :].rearrange("p (h t) -> p h t", h=4)).then_inc(s["d_u_ok"], 1)
                act.wait_ge(s["d_g"], c + 1)
                act.copy(ZG[:, :, HD:], ps[:, 6, :].rearrange("p (h t) -> p h t", h=AH)).then_inc(s["d_g_ok"], 1)
                for hf in range(2):
                    act.wait_ge(s["d_m"], 2 * c + hf + 1)
                    act.copy(M[:, 4 * hf:4 * hf + 4, :], ps[:, hf, :].rearrange("p (h t) -> p h t", h=4)).then_inc(s["d_m_ok"], 1)
                act.wait_ge(s["d_y"], c + 1)
                act.copy(YT[:, :, c * P:(c + 1) * P], ps[:, 5, :].rearrange("p (h t) -> p h t", h=HP)).then_inc(s["d_y_ok"], 1)
            act.wait_ge(s["sf_ps"], 1)
            act.copy(Sout, ps[0:HD, 6, :]).then_inc(s["sf_ok"], 1)
            act.wait_ge(s["d_y"], NT)
            act.activation(osq[:, :, 0:SEQ], pT[:, Q_:Q_ + GRP, 1:1 + SEQ], ACT.Square)
            for g in range(GRP):
                last = act.activation(by4(osq[:, g, SEQ:TOK]), sample4(pT[:, Q_ + g, 1 + SEQ:W]), ACT.Square)
            last.then_inc(s["f_sq"], 1)
            act.wait_ge(s["f_var"], 1)
            act.wait_ge(s["eps_ok"], 1)
            for n, (a, m) in enumerate(G512):
                last = act.activation(gms[:, a:a + m], ps[:, 3 + n, 0:m], ACT.Sqrt, scale=1.0 / (BH * HD), bias=eps[:, 0:1])
            last.then_inc(s["f_std"], 1)
            act.wait_ge(s["ys_ps"], 1)
            act.copy(yS[:, :, :], ps[:, 6, 0:HP * NS].rearrange("p (h t) -> p h t", h=HP)).then_inc(s["ys_ok"], 1)
            for hp in range(HP):
                act.wait_ge(s["f_yc"], hp + 1)
                if hp >= 1:
                    act.wait_ge(s["f_var"], 1 + hp)
                act.activation(gsq[:, 0:SEQ], YT[:, hp, :], ACT.Square)
                act.activation(gsq[:, SEQ:TOK], yS[:, hp, :], ACT.Square).then_inc(s["f_sq"], 1)
                act.wait_ge(s["f_var"], 1 + hp + 1)
                if hp >= 1:
                    act.wait_ge(s["f_mx"], 2 * GRP + 2 * hp)
                else:
                    act.wait_ge(s["ptail_out"], 16)
                for n, (a, m) in enumerate(G512):
                    last = act.activation(grs[:, a:a + m], ps[:, 3 + n, 0:m], ACT.Sqrt, bias=eps[:, 1:2])
                last.then_inc(s["f_std"], 1)
            for t in range(NTT):
                n = toks(t)
                act.wait_ge(s["g_x2"], t + 1)
                if t == 0:
                    act.wait_ge(s["f_mx"], 2 * GRP + 2 * HP)
                act.activation(sqj2[0:n, :], X2[0:n, t, :], ACT.Square, accum_out=stat[0:n, t:t + 1]).then_inc(s["sumsq"], 1)
                act.wait_ge(s["sumsq"], NTT + t + 1)
                act.activation(stat[0:n, 10 + t:11 + t], stat[0:n, t:t + 1], ACT.Sqrt, scale=1.0 / D, bias=eps[0:n, 0:1]).then_inc(s["std_ok"], 1)
                for j in range(2):
                    act.wait_ge(s["hT_ps"], 2 * NTT + 2 * t + j + 1)
                    if t >= 2:
                        act.wait_ge(s["g_lg"], t - 1)
                    act.copy(h2T[:, t % 2, 4 * j:4 * j + 4, 0:n], ps[:, 4 + j, 0:4 * n].rearrange("p (k c) -> p k c", k=4)).then_inc(s["hT_ok"], 1)
            act.wait_ge(s["r_dve"], 1)
            act.activation(rt_["gb"], rt_["ga"], ACT.Exp).then_inc(s["r_act"], 1)
            act.wait_ge(s["r_dve"], 2)
            act.activation(rt_["m2"], rt_["m2"], ACT.Exp).then_inc(s["r_act"], 1)

            def turned(g, a):
                for j in range(2):
                    act.wait_ge(s["xa_ps"], 2 * g + (j + 1))
                    act.copy(xgT[:, a, 4 * j:4 * j + 4, 0:P], ps[:, j, :].rearrange("p (k c) -> p k c", k=4)).then_inc(s["xa_ok"], 1)

            def silu(g, a, first):
                for f in range(4):
                    act.wait_ge(s["gu_ps"], 4 * g + (f + 1))
                    if not (first and f < 2):
                        act.wait_ge(s["ac_ok"], 4 * g + (f - 1))
                    act.activation(egl[:, f % 2, :], ps[:, 3 + f % 2, 0:CAP], ACT.Silu).then_inc(s["sl_ok"], 1)

            def rows_out(g, a, early):
                if not early:
                    act.wait_ge(s[f"yst{a}"], 16 * g)
                act.wait_ge(s["ya_ps"], 4 * g + 1)
                act.copy(eyA[:, a, 0:512], ps[:, 5, :]).then_inc(s["yo_act"], 1)
                act.wait_ge(s["ya_ps"], 4 * g + 3)
                act.copy(eyB[:, a, 0:512], ps[0:XB, 7, :]).then_inc(s["yo_act"], 1)

            def store(g, e, a):
                act.wait_ge(s["yo_act"], 2 * g + 2)
                act.wait_ge(s["yo_dve"], 2 * g + 2)
                act.dma_start(y_slots[e, 0:P, :], eyA[:, a, :]).then_inc(s[f"yst{a}"], 16)
                act.dma_start(y_slots[e, P:CAP, :], eyB[:, a, :]).then_inc(s[f"yst{a}"], 16)

            act.nop().then_inc(s["yst1"], 16)
            act.wait_ge(s["n_rounds"], 1)
            rounds = act.value_load(nround[0:1, 0:1], min_val=1, max_val=ROUNDS)
            with act.Fori(0, ROUNDS) as r:
                with act.If(rounds > r):
                    g0 = NE * r
                    turned(g0, 0)
                    silu(g0, 0, True)
                    turned(g0 + 1, 1)
                    rows_out(g0, 0, True)
                    silu(g0 + 1, 1, False)
                    store(g0, 0, 0)
                    with act.Fori(1, NE // 2) as q:
                        g = NE * r + 2 * q
                        turned(g, 0)
                        rows_out(g - 1, 1, False)
                        silu(g, 0, False)
                        store(g - 1, 2 * q - 1, 1)
                        turned(g + 1, 1)
                        rows_out(g, 0, False)
                        silu(g + 1, 1, False)
                        store(g, 2 * q, 0)
                    rows_out(g0 + (NE - 1), 1, False)
                    store(g0 + (NE - 1), NE - 1, 1)
                    act.wait_ge(s["yst0"], 16 * NE * (r + 1))
                    act.wait_ge(s["yst1"], 16 * NE * (r + 1) + 16)
                    act.nop().then_inc(s["rows_done"], 1)
                    act.wait_ge(s["round_done"], r + 1)
                    alone(act)
            for t in range(NTT):
                n = toks(t)
                act.activation(sqj2[0:n, :], X2[0:n, t, :], ACT.Square, accum_out=stat[0:n, t:t + 1]).then_inc(s["sumsq"], 1)
                act.wait_ge(s["sumsq"], 2 * NTT + t + 1)
                act.activation(stat[0:n, 10 + t:11 + t], stat[0:n, t:t + 1], ACT.Sqrt, scale=1.0 / D, bias=eps[0:n, 0:1]).then_inc(s["std_ok"], 1)

        @block.vector
        def _(dve):
            chain = [0]

            def link(ins):
                chain[0] += 1
                ins.then_inc(s["dve"], 1)
                dve.wait_ge(s["dve"], chain[0])

            def mix(pos, dst):
                c = SRC_BLOCK[pos]
                link(dve.tensor_tensor(dst, pT[:, pos, 0:W1], pT[:, pos, 1:W], ALU.subtract))
                return dve.scalar_tensor_tensor(dst, dst, V["mu_shift"][:, c:c + 1], pT[:, pos, 1:W], ALU.mult, ALU.add)

            def tail(a, b):
                dve.tensor_copy(tails[:, a:b, 0:1], pT[:, a:b, SEQ:SEQ + 1]).then_inc(s["tails_ok"], 1)
                dve.tensor_copy(tails[:, a:b, 1:], pT[:, a:b, SEQ + 1 + DT:W:DT + 1]).then_inc(s["tails_ok"], 1)

            for t in range(NT + 1):
                n = toks(t)
                dve.wait_ge(s["sumsq"], t + 1)
                dve.tensor_scalar(stat[0:n, 10 + t:11 + t], stat[0:n, t:t + 1], 1.0 / D, RMS_EPS, ALU.mult, ALU.add).then_inc(s["ms_ok"], 1)
                dve.wait_ge(s["std_ok"], t + 1)
                link(dve.reciprocal(stat[0:n, 30 + t:31 + t], stat[0:n, 20 + t:21 + t]))
                dve.tensor_scalar(xt[0:n, t % 2, :], xt[0:n, t % 2, :], stat[0:n, 30 + t:31 + t], None, ALU.mult).then_inc(s["h_ok"], 1)
                if t == 0:
                    dve.wait_ge(s["vec_ok"], 1)
                for j in range(2):
                    dve.wait_ge(s["hT_ps"], 2 * t + j + 1)
                    g = V["norm_mix_g"][:, 4 * j:4 * j + 4]
                    src = ps[:, 2 * (t % 2) + j, 0:4 * n].rearrange("p (k c) -> p k c", k=4)
                    dst = cols(hT[:, 4 * j:4 * j + 4, :], t)
                    if t < NT:
                        dve.tensor_tensor(dst, src, g[:, :, None].to_broadcast([P, 4, n]), ALU.mult).then_inc(s["hT_ok"], 1)
                    else:
                        for k in range(4):
                            last = dve.tensor_scalar(dst[:, k], src[:, k].rearrange("p (b t) -> p b t", t=DT), g[:, k:k + 1], None, ALU.mult)
                        last.then_inc(s["hT_ok"], 1)
            link(dve.tensor_scalar(omka[:, :], V["k_a"], -1.0, 1.0, ALU.mult, ALU.add))
            dve.wait_ge(s["prev_ok"], 2)
            tail(12, 14)
            mix(LORA, kt).then_inc(s["mixed"], 1)
            mix(GD, rt).then_inc(s["mixed"], 1)
            for hp in range(HP):
                if hp == 0:
                    dve.wait_ge(s["lora_act"], 3)
                else:
                    dve.wait_ge(s["smp_ps"], 2 * hp)
                    dve.wait_ge(s["scaled"], 2 * hp)
                for pos, dst in ((K_(hp), kt), (R_(hp), rt), (V_(hp), vM[:, hp, :])):
                    dve.wait_ge(s["prev_ok"], PSLOT[pos] + 1)
                    mix(pos, dst).then_inc(s["mixed"], 1)
                if hp == 0:
                    dve.wait_ge(s["prev_ok"], 14)
                    tail(0, 12)
                dve.wait_ge(s["kk_ps"], hp + 1)
                for g, (a, m) in enumerate(G3B):
                    last = dve.tensor_scalar(rn[:, a:a + m], ps[:, g, 0:m], 1e-24, None, ALU.max)
                last.then_inc(s["kk_ms"], 1)
                dve.wait_ge(s["gates_ok"], 2 * hp + 1)
                for c in range(NT):
                    last = dve.tensor_tensor_scan(cc[:, c * P:(c + 1) * P], T["ones"], sw[:, c * P:(c + 1) * P], 0.0, ALU.mult, ALU.add)
                link(last)
                c3 = cc[:, 0:SEQ].rearrange("p (c t) -> p c t", t=P)
                link(dve.tensor_copy(gam[:, 0, hp, :], c3[:, :, P // 2 - 1]))
                link(dve.tensor_tensor(c3, c3, gam[:, 0, hp, :][:, :, None].to_broadcast([P, NT, P]), ALU.subtract))
                dve.tensor_copy(gam[:, 1, hp, :], c3[:, :, P - 1])
                dve.tensor_tensor(cex[:, 0:SEQ], cc[:, 0:SEQ], sw[:, 0:SEQ], ALU.subtract).then_inc(s["cum_ok"], 1)
                dve.wait_ge(s["kk_std"], hp + 1)
                link(dve.reciprocal(rn, rn))
                link(dve.scalar_tensor_tensor(kk, kt, V["k_k"][:, hp:hp + 1], rn, ALU.mult, ALU.mult))
                dve.wait_ge(s["gates_ok"], 2 * hp + 2)
                link(dve.scalar_tensor_tensor(bb, kk, -1.0, sa, ALU.mult, ALU.mult))
                link(dve.tensor_scalar(fac, sa, V["k_a"][:, hp:hp + 1], omka[:, hp:hp + 1], ALU.mult, ALU.add))
                link(dve.tensor_tensor(kt, kt, fac, ALU.mult))
                dve.scalar_tensor_tensor(rk, rt, V["r_k"][:, hp:hp + 1], kt, ALU.mult, ALU.mult).then_inc(s["bonus_in"], 1)
                dve.wait_ge(s["exps"], 4 * hp + 4)
                dve.tensor_tensor(NBT[:, hp, :], bb[:, 0:SEQ], pinv[:, 0:SEQ], ALU.mult).then_inc(s["smp_in"], 1)
                link(dve.tensor_tensor(KBT[:, hp, :], kt[:, 0:SEQ], pinv[:, 0:SEQ], ALU.mult))
                dve.wait_ge(s["bonus_ps"], hp + 1)
                for g, (a, m) in enumerate(G3B):
                    last = dve.tensor_tensor(BV[:, hp, a:a + m], ps[:, 3 + g, 0:m], vM[:, hp, a:a + m], ALU.mult)
                last.then_inc(s["blk_done"], 1)
            dve.tensor_tensor(gam[:, 1, :, 0:NT - 1], gam[:, 1, :, 0:NT - 1], gam[:, 0, :, 1:NT], ALU.add).then_inc(s["gam_ok"], 1)

            five = lambda ap: ap.rearrange("p (b t) -> p b t", t=DT + 1)[:, :, 1:]
            four = lambda ap: ap.rearrange("p (b t) -> p b t", t=DT)
            dve.wait_ge(s["p_ok"], 20)
            for n, pos in enumerate((KK_, VV_)):
                last = dve.tensor_copy(four(kvs[:, n, :]), five(pT[:, pos, 1 + SEQ:W]))
            for g in range(GRP):
                last = dve.tensor_copy(four(qs[:, g * NS:(g + 1) * NS]), five(pT[:, Q_ + g, 1 + SEQ:W]))
            last.then_inc(s["kvs_ok"], 1)
            dve.wait_ge(s["bias_in"], 16 * 5)
            dve.wait_ge(s["sa_pe"], 4)
            link(dve.scalar_tensor_tensor(ssc.rearrange("p v k -> p (v k)"), ps[:, 6, 0:320], HD ** -0.5, sbias.rearrange("p v k -> p (v k)"), ALU.mult, ALU.add))
            link(dve.tensor_reduce(ast[:, 40:42], ssc, AX.X, ALU.max))
            link(dve.tensor_tensor(ast[:, 40:42], ast[:, 40:42], sinks, ALU.max))
            link(dve.tensor_scalar(ast[:, 32:34], ast[:, 40:42], -1.0, None, ALU.mult))
            dve.tensor_tensor(ast[:, 38:40], sinks, ast[:, 32:34], ALU.add).then_inc(s["sa_dve"], 1)
            dve.wait_ge(s["sa_act"], 5)
            link(dve.tensor_tensor(ast[:, 42:44], ast[:, 34:36], ast[:, 36:38], ALU.add))
            link(dve.reciprocal(ast[:, 44:46], ast[:, 42:44]))
            dve.tensor_tensor(ssc, ssc, ast[:, 44:46][:, :, None].to_broadcast([P, 2, 160]), ALU.mult).then_inc(s["sa_dve"], 1)
            for t in range(NT):
                nk = 1 if t == 0 else 2
                dve.wait_ge(s["sc_ps"], t + 1)
                if t:
                    dve.wait_ge(s["pt_ps"], 4 * t)
                for b in range(4):
                    src = ps[:, b, :].rearrange("p (h k) -> p h k", h=2)[:, :, 0:nk * P]
                    last = dve.scalar_tensor_tensor(sc[:, 2 * b:2 * b + 2, 0:nk * P], src, HD ** -0.5, abias[:, 2 * b:2 * b + 2, 2 * P - nk * P:], ALU.mult, ALU.add)
                last.then_inc(s["sc_ok"], 1)
                dve.wait_ge(s["sc_ok"], t + 1)
                link(dve.tensor_reduce(ast[:, 48:56], sc[:, :, 0:nk * P], AX.X, ALU.max))
                link(dve.tensor_tensor(ast[:, 48:56], ast[:, 48:56], sinkb, ALU.max))
                link(dve.tensor_scalar(ast[:, 0:8], ast[:, 48:56], -1.0, None, ALU.mult))
                dve.tensor_tensor(ast[:, 24:32], sinkb, ast[:, 0:8], ALU.add).then_inc(s["m_ok"], 1)
                dve.wait_ge(s["e_ok"], t + 1)
                link(dve.tensor_tensor(ast[:, 8:16], ast[:, 8:16], ast[:, 16:24], ALU.add))
                link(dve.reciprocal(ast[:, 56:64], ast[:, 8:16]))
                dve.tensor_tensor(sc[:, :, 0:nk * P], sc[:, :, 0:nk * P], ast[:, 56:64][:, :, None].to_broadcast([P, BH, nk * P]), ALU.mult).then_inc(s["p_norm"], 1)
            def lm(lv, tr):
                k = 2 * lv + tr
                return level[:, k * P:(k + 1) * P][:, None, :].to_broadcast([P, 4, P])

            masks = table[:, 3 * P:5 * P].rearrange("p (two t) -> p two t", two=2)
            dve.wait_ge(s["win_out"], 16 * 6)
            for c in range(NT):
                dve.wait_ge(s["d_t"], 4 * c + 2)
                dve.tensor_copy(ZG[:, :, 0:HD], ps[:, 1, :].rearrange("p (h t) -> p h t", h=AH)).then_inc(s["d_t_dve"], 1)
                dve.wait_ge(s["d_t"], 4 * c + 4)
                dve.tensor_copy(Bt, ps[:, 3, :]).then_inc(s["d_t_dve"], 1)
                if c == 0:
                    dve.wait_ge(s["level_ok"], 1)
                for hf in range(2):
                    for n, (dst, name) in enumerate(((LB, "d_lb"), (LK, "d_lk"))):
                        dve.wait_ge(s[name], 2 * c + hf + 1)
                        for b in range(2):
                            h = 4 * hf + b
                            last = dve.tensor_tensor(dst[:, h:h + 3:2, :, :].rearrange("p h two t -> p h (two t)"),
                                                     ps[:, 4 + 2 * n + b, :].rearrange("p (h m) -> p h m", h=2),
                                                     table[:, 3 * P:5 * P][:, None, :].to_broadcast([P, 2, 2 * P]), ALU.mult)
                        last.then_inc(s[name + "_ok"], 1)
                dve.wait_ge(s["d_lc"], c + 1)
                dve.wait_ge(s["d_eye"], 2 * c + 2)
                dve.wait_ge(s["d_lb_ok"], 2 * c + 2)
                for e in range(2):
                    hs = slice(e, AH, 2)
                    dve.copy_predicated(TL[:, hs, :], lm(0, 0), ps[:, e, :].rearrange("p (h t) -> p h t", h=4)).then_inc(s["d_lc_ok"], 1)
                    dve.copy_predicated(TT[:, hs, :], lm(0, 1), LB[:, hs, 0, :]).then_inc(s["d_lc_ok"], 1)
                for lv in range(1, LV):
                    for hf in range(2):
                        n = 2 * ((LV - 1) * c + lv - 1) + hf
                        hs = slice(4 * hf, 4 * hf + 4)
                        dve.wait_ge(s["d_x"], n + 1)
                        dve.copy_predicated(TL[:, hs, :], lm(lv, 0), ps[:, 2 + hf, :].rearrange("p (h t) -> p h t", h=4)).then_inc(s["d_x_ok"], 1)
                        dve.wait_ge(s["d_xt"], n + 1)
                        dve.copy_predicated(TT[:, hs, :], lm(lv, 1), ps[:, 4 + hf, :].rearrange("p (h t) -> p h t", h=4)).then_inc(s["d_xt_ok"], 1)
                dve.wait_ge(s["d_re"], c + 1)
                if c >= 1:
                    dve.wait_ge(s["d_y"], c)
                dve.tensor_tensor(Re, ps[:, 2, :].rearrange("p (h t) -> p h t", h=HP), ZR[:, :, c, 1, :], ALU.add).then_inc(s["d_re_ok"], 1)
                dve.wait_ge(s["d_a"], c + 1)
                dve.tensor_tensor(AT, ps[:, 3, 0:HP * HD].rearrange("p (h t) -> p h t", h=HP), T["eye64"][:, None, :].to_broadcast([P, HP, HD]),
                                  ALU.add).then_inc(s["d_a_ok"], 1)
                if c == 0:
                    dve.wait_ge(s["gamma_ok"], 1)
                dve.wait_ge(s["d_s"], c + 1)
                dve.wait_ge(s["d_y"], c + 1)
                dve.tensor_tensor(Sb, ps[:, 4, 0:HP * HD].rearrange("p (h t) -> p h t", h=HP), gamma[:, :, c:c + 1].to_broadcast([P, HP, HD]),
                                  ALU.mult).then_inc(s["d_s_ok"], 1)

            dve.memset(eps[:, 0:1], RMS_EPS)
            dve.memset(eps[:, 1:2], LNX_EPS).then_inc(s["eps_ok"], 1)
            dve.wait_ge(s["f_std"], 1)
            link(dve.reciprocal(gms[:, 0:TOK], gms[:, 0:TOK]))
            for g in range(GRP):
                dve.scalar_tensor_tensor(MX[:, 4 + g, 0:SEQ], pT[:, Q_ + g, 1:1 + SEQ], V["attn_norm_g"][:, g:g + 1], gms[:, 0:SEQ], ALU.mult, ALU.mult)\
                   .then_inc(s["f_mx"], 1)
                dve.scalar_tensor_tensor(by4(MX[:, 4 + g, SEQ:TOK]), sample4(pT[:, Q_ + g, 1 + SEQ:W]), V["attn_norm_g"][:, g:g + 1],
                                         by4(gms[:, SEQ:TOK]), ALU.mult, ALU.mult).then_inc(s["f_mx"], 1)
            for hp in range(HP):
                dve.wait_ge(s["f_mean"], hp + 1)
                dve.tensor_tensor(YT[:, hp, :], YT[:, hp, :], ps[:, 0:2, :].rearrange("p b c -> p (b c)"), ALU.subtract)
                dve.tensor_tensor(yS[:, hp, :], yS[:, hp, :], ps[:, 2, 0:NS], ALU.subtract).then_inc(s["f_yc"], 1)
                dve.wait_ge(s["f_yc"], hp + 1)
                dve.wait_ge(s["f_std"], 1 + hp + 1)
                link(dve.reciprocal(grs[:, 0:TOK], grs[:, 0:TOK]))
                g, b = V["lnx_g"][:, hp:hp + 1], V["lnx_b"][:, hp:hp + 1]
                dst, dsts = MX[:, hp, 0:SEQ], MX[:, hp, SEQ:TOK]
                dve.scalar_tensor_tensor(dst, YT[:, hp, :], g, grs[:, 0:SEQ], ALU.mult, ALU.mult)
                link(dve.scalar_tensor_tensor(dsts, yS[:, hp, :], g, grs[:, SEQ:TOK], ALU.mult, ALU.mult))
                dve.scalar_tensor_tensor(dst, dst, b, BV[:, hp, 0:SEQ], ALU.add, ALU.add)
                link(dve.scalar_tensor_tensor(by4(dsts), by4(dsts), b, sample4(BV[:, hp, SEQ:W1]), ALU.add, ALU.add))
                dve.wait_ge(s["f_gate"], hp + 1)
                dve.tensor_tensor(dst, dst, ps[:, 6:8, :].rearrange("p b c -> p (b c)"), ALU.mult).then_inc(s["f_mx"], 1)
                dve.tensor_tensor(dsts, dsts, ps[:, 5, NS:2 * NS], ALU.mult).then_inc(s["f_mx"], 1)
            dve.wait_ge(s["x2_in"], 32)
            for t in range(NTT):
                n = toks(t)
                dve.wait_ge(s["g_ps"], t + 1)
                dve.tensor_tensor(X2[0:n, t, :], X2[0:n, t, :], ps[0:n, 2 * (t % 2):2 * (t % 2) + 2, :].rearrange("p b c -> p (b c)"), ALU.add)\
                   .then_inc(s["g_x2"], 1)
                dve.wait_ge(s["g_x2"], t + 1)
                dve.wait_ge(s["std_ok"], NTT + t + 1)
                if t == 0:
                    dve.wait_ge(s["g_in"], 16 * 6)
                if t >= 2:
                    dve.wait_ge(s["hT_ps"], 2 * NTT + 2 * (t - 1))
                    dve.wait_ge(s[f"h2o{t % 2}"], 16 * (t // 2))
                link(dve.reciprocal(stat[0:n, 20 + t:21 + t], stat[0:n, 10 + t:11 + t]))
                dve.scalar_tensor_tensor(h2[0:n, t % 2, :], X2[0:n, t, :], stat[0:n, 20 + t:21 + t], gffn[0:n, :], ALU.mult, ALU.mult).then_inc(s["h_ok"], 1)
            X = rt_
            by = lambda n, k: X[n].rearrange("p (t k) -> p t k", k=k)
            wide = lambda ap, k: ap[:, :, None].to_broadcast([P, NTT, k])
            lg = by("lg", 20)
            first4 = T["iota"][:, 0:4][:, None, :].to_broadcast([P, NTT, 4])

            def first_max(src, top, out, tmp):
                link(dve.tensor_tensor(tmp, src, wide(top, 4), ALU.is_equal))
                link(dve.scalar_tensor_tensor(out, first4, -4.0, tmp, ALU.add, ALU.mult))
                link(dve.tensor_reduce(X["den"], out, AX.X, ALU.min))
                link(dve.tensor_tensor(out, out, wide(X["den"], 4), ALU.is_equal))

            link(dve.memset(lg[:, NT, :], 0.0))
            dve.wait_ge(s["g_lg"], NTT)
            link(dve.tensor_tensor(lg[:, 0:NT, :], ps[:, 6, 0:NT * 20].rearrange("p (t k) -> p t k", k=20), rbias[:, None, :].to_broadcast([P, NT, 20]), ALU.add))
            link(dve.tensor_tensor(lg[0:NS, NT, :], ps[0:NS, 6, NT * 20:NTT * 20], rbias[0:NS, :], ALU.add))
            link(dve.tensor_reduce(X["m"], lg[:, :, 0:NG], AX.X, ALU.max))
            dve.tensor_tensor(by("ga", 4), lg[:, :, 0:NG], wide(X["m"], 4), ALU.subtract).then_inc(s["r_dve"], 1)
            first_max(lg[:, :, 0:NG], X["m"], by("ohg", 4), by("oh2", 4))
            le = lg[:, :, NG:].rearrange("p t (g j) -> p t g j", g=NG)
            pr = X["prod"].rearrange("p (t g j) -> p t g j", t=NTT, g=NG)
            leg, oh1, oh2 = by("leg", 4), by("oh1", 4), by("oh2", 4)
            link(dve.tensor_tensor(pr, le, by("ohg", 4)[:, :, :, None].to_broadcast([P, NTT, NG, EPG]), ALU.mult))
            link(dve.tensor_reduce(leg, pr.rearrange("p t g j -> p t j g"), AX.X, ALU.add))
            link(dve.tensor_reduce(X["m1"], leg, AX.X, ALU.max))
            first_max(leg, X["m1"], oh1, oh2)
            link(dve.scalar_tensor_tensor(leg, oh1, -1e30, leg, ALU.mult, ALU.add))
            link(dve.tensor_reduce(X["m2"], leg, AX.X, ALU.max))
            dve.wait_ge(s["r_act"], 1)
            first_max(leg, X["m2"], oh2, by("ga", 4))
            dve.tensor_tensor(X["m2"], X["m2"], X["m1"], ALU.subtract).then_inc(s["r_dve"], 1)
            link(dve.tensor_reduce(X["gw"], by("gb", 4), AX.X, ALU.add))
            for name, oh in (("OH1", oh1), ("OH2", oh2)):
                O = X[name].rearrange("p (t g j) -> p t g j", t=NTT, g=NG)
                link(dve.tensor_tensor(O, by("ohg", 4)[:, :, :, None].to_broadcast([P, NTT, NG, EPG]),
                                       oh[:, :, None, :].to_broadcast([P, NTT, NG, EPG]), ALU.mult))
                link(dve.tensor_tensor(by(name, NE), by(name, NE), wide(T["valid"], NE), ALU.mult))
            dve.tensor_tensor(X["OHs"], X["OH1"], X["OH2"], ALU.add).then_inc(s["r_dve"], 1)
            dve.wait_ge(s["r_act"], 2)
            link(dve.tensor_scalar(X["den"], X["m2"], 1.0, None, ALU.add))
            link(dve.tensor_tensor(X["den"], X["den"], X["gw"], ALU.mult))
            link(dve.reciprocal(wts2[:, 0, :], X["den"]))
            link(dve.tensor_tensor(wts2[:, 1, :], wts2[:, 0, :], X["m2"], ALU.mult))
            dve.wait_ge(s["r_pe"], 1)
            link(dve.tensor_copy(X["rank"], ps[:, 7, 0:NTT * NE]))
            link(dve.tensor_copy(X["tot"], ps[:, 7, NTT * NE:2 * NTT * NE]))
            rank, tot = by("rank", NE), by("tot", NE)
            link(dve.memset(X["cnt"], 0.0))
            for t in range(NTT):
                link(dve.tensor_tensor(rank[:, t, :], rank[:, t, :], X["cnt"], ALU.add))
                link(dve.tensor_tensor(X["cnt"], X["cnt"], tot[:, t, :], ALU.add))
            for k, name in enumerate(("OH1", "OH2")):
                ks = slice(k * NTT, (k + 1) * NTT)
                link(dve.tensor_tensor(by("prod", NE), by(name, NE), rank, ALU.mult))
                link(dve.tensor_reduce(X["rk"][:, ks], by("prod", NE), AX.X, ALU.add))
                link(dve.tensor_tensor(by("prod", NE), by(name, NE), T["iota"][:, 0:NE][:, None, :].to_broadcast([P, NTT, NE]), ALU.mult))
                link(dve.tensor_reduce(X["ei"][:, ks], by("prod", NE), AX.X, ALU.add))
                link(dve.tensor_tensor(X["OHT"][:, k * NTT * NE:(k + 1) * NTT * NE].rearrange("p (t e) -> p t e", e=NE), by(name, NE), wide(T["tokid"], NE), ALU.mult))
            link(dve.tensor_reduce(X["mc"], X["cnt"], AX.X, ALU.max))
            link(dve.tensor_scalar(X["ei"], X["ei"], float(CAP), None, ALU.mult))
            link(dve.memset(X["nr"], 1.0))
            for j in range(1, ROUNDS):
                link(dve.tensor_scalar(X["cmp"], X["mc"], float(CAP * j), None, ALU.is_gt))
                link(dve.tensor_tensor(X["nr"], X["nr"], X["cmp"], ALU.add))
            dve.tensor_copy(nround[:, :], X["nr"]).then_inc(s["n_rounds"], 1)

            def turned(g, a):
                dve.wait_ge(s["xb_ps"], g + 1)
                dve.tensor_copy(xgT[:, a, :, P:CAP], ps[:, 2, 0:KB * XB].rearrange("p (k c) -> p k c", k=KB)).then_inc(s["xb_ok"], 1)

            def product(g, a):
                for f in range(4):
                    dve.wait_ge(s["sl_ok"], 4 * g + (f + 1))
                    dve.tensor_tensor(eact[:, a, f, :], egl[:, f % 2, :], ps[:, 3 + f % 2, CAP:2 * CAP], ALU.mult).then_inc(s["ac_ok"], 1)

            def rows_out(g, a, early):
                if not early:
                    dve.wait_ge(s[f"yst{a}"], 16 * g)
                dve.wait_ge(s["ya_ps"], 4 * g + 2)
                dve.tensor_copy(eyA[:, a, 512:], ps[:, 6, :]).then_inc(s["yo_dve"], 1)
                dve.wait_ge(s["ya_ps"], 4 * g + 4)
                dve.tensor_copy(eyB[:, a, 512:], ps[0:XB, 5, :]).then_inc(s["yo_dve"], 1)

            dve.wait_ge(s["n_rounds"], 1)
            rounds = dve.value_load(nround[0:1, 0:1], min_val=1, max_val=ROUNDS)
            with dve.Fori(0, ROUNDS) as r:
                with dve.If(rounds > r):
                    steps = [0]

                    def again(ins):
                        steps[0] += 1
                        ins.then_inc(s["dve_r"], 1)
                        dve.wait_ge(s["dve_r"], STEPS * r + steps[0])

                    for m in range(2 * NTT):
                        if m >= 2:
                            dve.wait_ge(s["hot_ps"], 2 * NTT * r + m - 1)
                        dve.tensor_scalar(hot[:, m % 2, :], T["iota"], X["rk"][:, m:m + 1], None, ALU.is_equal).then_inc(s["hot"], 1)
                    dve.wait_ge(s["hot_ps"], 2 * NTT * r + 2 * NTT)
                    dve.tensor_copy(idxA[:, :], ps[:, 7, 0:NE])
                    dve.tensor_copy(idxB[0:XB, :], ps[0:XB, 6, 0:NE]).then_inc(s["i_ok"], 1)
                    again(dve.tensor_scalar(X["ov"], X["rk"], float(CAP), None, ALU.is_lt))
                    again(dve.scalar_tensor_tensor(X["ov"], X["rk"], 0.0, X["ov"], ALU.is_ge, ALU.mult))
                    again(dve.tensor_tensor(X["pos"], X["ei"], X["rk"], ALU.add))
                    again(dve.tensor_tensor(X["pos"], X["pos"], X["ov"], ALU.mult))
                    dve.tensor_copy(posi.rearrange("p k t -> p (k t)"), X["pos"]).then_inc(s["pos_ok"], 1)
                    dve.tensor_tensor(wtr.rearrange("p k t -> p (k t)"), wts2.rearrange("p k t -> p (k t)"), X["ov"], ALU.mult)
                    dve.wait_ge(s["hot"], 2 * NTT * r + 2 * NTT)
                    dve.tensor_scalar(X["rk"], X["rk"], float(-CAP), None, ALU.add)
                    g0 = NE * r
                    turned(g0, 0)
                    product(g0, 0)
                    turned(g0 + 1, 1)
                    rows_out(g0, 0, True)
                    product(g0 + 1, 1)
                    with dve.Fori(1, NE // 2) as q:
                        g = NE * r + 2 * q
                        turned(g, 0)
                        rows_out(g - 1, 1, False)
                        product(g, 0)
                        turned(g + 1, 1)
                        rows_out(g, 0, False)
                        product(g + 1, 1)
                    rows_out(g0 + (NE - 1), 1, False)
                    for t in range(NTT):
                        n = toks(t)
                        dve.wait_ge(s[f"c{t % 2}"], 32 * (NTT // 2 + 1 - t % 2) * r + 32 * (t // 2 + 1))
                        again(dve.scalar_tensor_tensor(X2[0:n, t, :], cy[0:n, t, 0, :], wtr[0:n, 0, t:t + 1], X2[0:n, t, :], ALU.mult, ALU.add))
                        again(dve.scalar_tensor_tensor(X2[0:n, t, :], cy[0:n, t, 1, :], wtr[0:n, 1, t:t + 1], X2[0:n, t, :], ALU.mult, ALU.add))
                    assert steps[0] == STEPS
                    dve.nop().then_inc(s["round_done"], 1)
                    dve.wait_ge(s["round_done"], r + 1)
                    alone(dve)
            def final(t):
                n = toks(t)
                dve.wait_ge(s["std_ok"], 2 * NTT + t + 1)
                link(dve.reciprocal(stat[0:n, 20 + t:21 + t], stat[0:n, 10 + t:11 + t]))
                dve.scalar_tensor_tensor(cy[0:n, t, 0, :], X2[0:n, t, :], stat[0:n, 20 + t:21 + t], gfin[0:n, :], ALU.mult, ALU.mult).then_inc(s["fin"], 1)

            for t in range(NTT):
                final(t)

        @block.gpsimd
        def _(pool):
            pool.memset(hT[:, :, 0:1], 0.0)
            pool.memset(hT[:, :, 1 + SEQ:W:DT + 1], 0.0).then_inc(s["pad_zero"], 1)
            for hp in range(HP):
                pool.wait_ge(s["smp_in"], hp + 1)
                pool.tensor_tensor(ZR[:, hp, :, 0, :], kk[:, 0:SEQ].rearrange("p (c t) -> p c t", t=P),
                                   cex[:, 0:SEQ].rearrange("p (c t) -> p c t", t=P), ALU.mult).then_inc(s["scaled"], 1)
                pool.tensor_tensor(ZR[:, hp, :, 1, :], rt[:, 0:SEQ].rearrange("p (c t) -> p c t", t=P),
                                   cc[:, 0:SEQ].rearrange("p (c t) -> p c t", t=P), ALU.mult).then_inc(s["scaled"], 1)
            pool.wait_ge(s["level_in"], 16)
            pool.tensor_copy(level[:, :], levelf).then_inc(s["level_ok"], 1)
            chain = [0]

            def link(ins):
                chain[0] += 1
                ins.then_inc(s["pool"], 1)
                pool.wait_ge(s["pool"], chain[0])

            pool.wait_ge(s["sv_in"], 16 * 2 * DB)
            pool.wait_ge(s["st_in"], 32)
            pool.wait_ge(s["win_out"], 16 * 6)
            pool.wait_ge(s["ob_ok"], NT)

            def sum_keys(dst):
                m = HD // 2
                while m > 1:
                    link(pool.tensor_tensor(stm[:, :, 0:m], stm[:, :, 0:m], stm[:, :, m:2 * m], ALU.add))
                    m //= 2
                link(pool.tensor_tensor(dst, stm[:, :, 0:1], stm[:, :, 1:2], ALU.add))

            for t in range(DT):
                row = lambda a: svv[:, t, a, :][:, None, :].to_broadcast([P, HD // 2, HD])
                link(pool.tensor_tensor(stm, sst, row(0), ALU.mult))
                pool.tensor_tensor(sst, sst, row(3), ALU.mult)
                sum_keys(ssa[:, :, None])
                link(pool.tensor_tensor(stm, row(1), ssa[:, :, None].to_broadcast([P, HD // 2, HD]), ALU.mult))
                link(pool.tensor_tensor(sst, sst, stm, ALU.add))
                for vh in range(2):
                    q = slice(vh * HD, (vh + 1) * HD)
                    v = svv[q, t, 5, vh * (HD // 2):(vh + 1) * (HD // 2)]
                    last = pool.tensor_tensor(stm[q], svv[q, t, 2, :][:, None, :].to_broadcast([HD, HD // 2, HD]), v[:, :, None].to_broadcast([HD, HD // 2, HD]), ALU.mult)
                link(last)
                link(pool.tensor_tensor(sst, sst, stm, ALU.add))
                link(pool.tensor_tensor(stm, sst, row(4), ALU.mult))
                sum_keys(sy[:, t, :, None])
            pool.nop().then_inc(s["sr_ok"], 1)
            def gather(dst, src, idx):
                return pool.indirect_dma_start(dst, None, src, bass.IndirectOffsetOnAxis(idx, 0))

            pool.wait_ge(s["h2o0"], 16 * 5)
            pool.wait_ge(s["h2o1"], 16 * 4)
            pool.wait_ge(s["n_rounds"], 1)
            rounds = pool.value_load(nround[0:1, 0:1], min_val=1, max_val=ROUNDS)
            with pool.Fori(0, ROUNDS) as r:
                with pool.If(rounds > r):
                    pool.wait_ge(s["i_ok"], r + 1)
                    for e in range(NE):
                        if e >= 2:
                            pool.wait_ge(s["xb_ps"], NE * r + (e - 1))
                        alone(pool)
                        gather(xgA[:, e % 2, :], h2_dram, idxA[:, e:e + 1]).then_inc(s[f"xg{e % 2}"], 16)
                        gather(xgB[:, e % 2, :], h2_dram, idxB[0:XB, e:e + 1]).then_inc(s[f"xg{e % 2}"], 16)
                    pool.wait_ge(s["pos_ok"], r + 1)
                    pool.wait_ge(s["rows_done"], r + 1)
                    for t in range(NTT):
                        n = toks(t)
                        if t >= 2:
                            pool.wait_ge(s[f"c{t % 2}"], 32 * (NTT // 2 + 1 - t % 2) * r + 32 * (t // 2))
                        alone(pool)
                        for k in range(2):
                            gather(cy[0:n, t, k, :], y_dram, posi[0:n, k, t:t + 1]).then_inc(s[f"c{t % 2}"], 16)
                    pool.wait_ge(s["round_done"], r + 1)
                    alone(pool)


def kernel(**inputs):
    import concourse.bacc as bacc
    from concourse.bass_utils import run_bass_kernel_spmd

    nc = bacc.Bacc("TRN2", target_bir_lowering=False, num_devices=1)
    arrays, ins, outs = {}, {}, {}
    for name, a in {**inputs, **constants()}.items():
        a = np.ascontiguousarray(a)
        arrays[f"in_{name}"] = a
        ins[name] = nc.dram_tensor(f"in_{name}", a.shape, mybir.dt.from_np(a.dtype), kind="ExternalInput").ap()
    shapes = {
        "y_prompt": (1, SEQ, D), "y_sample": (DB, DT, D),
        "state_rwkv_prompt": (1, 1, AH, HD, HD), "state_shift_prompt": (1, 1, SHIFT_W),
        "cache_win_k_prompt": (1, 1, WIN, BKV, HD), "cache_win_v_prompt": (1, 1, WIN, BKV, HD),
        "state_rwkv_sample": (1, DB, AH, HD, HD), "state_shift_sample": (1, DB, SHIFT_W),
        "cache_win_k_sample": (1, DB, WIN, BKV, HD), "cache_win_v_sample": (1, DB, WIN, BKV, HD),
    }
    for name, shape in shapes.items():
        outs[name] = nc.dram_tensor(f"out_{name}", shape, F32, kind="ExternalOutput").ap()
    program(nc, ins, outs)
    r = run_bass_kernel_spmd(nc, [arrays], core_ids=[0])
    return tuple(r.results[0][f"out_{name}"] for name in shapes)
```
